# Optimizing a Trainium2 kernel written in Bass

```python
import jax, jax.numpy as jnp
from jax import lax
import numpy as np
import math
import jax
import jax.numpy as jnp

D_MODEL = 1024
BATCH = 1
SEQ = 256
DEPTH = 1

CHUNK = 64
Q_BLOCK = 128
SB_HEADS = 8
SB_HEAD_DIM = 64
SB_WIDTH = SB_HEADS * SB_HEAD_DIM
HG_HEADS = 4
HG_HEAD_DIM = 128
HG_WIDTH = HG_HEADS * HG_HEAD_DIM
N_BRANCH = 2
D_FF = 4 * D_MODEL
IN_COLS = 3 * SB_WIDTH + 4 * HG_WIDTH + N_BRANCH * D_MODEL
EPS = 1e-6


def rmsnorm(x, g):
    xf = x.astype(jnp.float32)
    y = xf * lax.rsqrt(jnp.mean(xf * xf, axis=-1, keepdims=True) + EPS)
    return y * g.astype(jnp.float32)

def split_heads(t, n_heads):
    b, s, w = t.shape
    return t.reshape(b, s, n_heads, w // n_heads).transpose(0, 2, 1, 3)

def merge_heads(t):
    b, h, s, d = t.shape
    return t.transpose(0, 2, 1, 3).reshape(b, s, h * d)

def stick_breaking_attention(q, k, v):
    b, h, s, dh = q.shape
    nb = s // Q_BLOCK
    scale = dh ** -0.5
    qb = q.reshape(b, h, nb, Q_BLOCK, dh).transpose(2, 0, 1, 3, 4)
    kpos = jnp.arange(s)

    def block(args):
        qi, i = args
        qpos = i * Q_BLOCK + jnp.arange(Q_BLOCK)
        z = jnp.einsum('bhqd,bhkd->bhqk', qi, k) * scale
        mask = kpos[None, :] < qpos[:, None]
        log_beta = jax.nn.log_sigmoid(z)
        log_rem = jnp.where(mask, log_beta - z, 0.0)
        between = lax.cumsum(log_rem, axis=3, reverse=True) - log_rem
        w = jnp.where(mask, jnp.exp(log_beta + between), 0.0)
        return jnp.einsum('bhqk,bhkd->bhqd', w, v)

    out = lax.map(block, (qb, jnp.arange(nb)))
    return out.transpose(1, 2, 0, 3, 4).reshape(b, h, s, dh)

def hgrn2_chunkwise(q, k, v, log_f):
    b, h, s, dk = q.shape
    dv = v.shape[-1]
    nc = s // CHUNK

    def to_chunks(t):
        return t.reshape(b, h, nc, CHUNK, t.shape[-1]).transpose(2, 0, 1, 3, 4)

    qc, kc, vc, gc = to_chunks(q), to_chunks(k), to_chunks(v), to_chunks(log_f)
    causal = jnp.arange(CHUNK)[:, None] >= jnp.arange(CHUNK)[None, :]

    def step(state, inp):
        qi, ki, vi, gi = inp
        bcum = jnp.cumsum(gi, axis=2)
        diff = bcum[:, :, :, None, :] - bcum[:, :, None, :, :]
        decay = jnp.exp(jnp.where(causal[:, :, None], diff, -jnp.inf))
        scores = jnp.einsum('bhtd,bhsd,bhtsd->bhts', qi, ki, decay)
        o = jnp.einsum('bhts,bhse->bhte', scores, vi) \
            + jnp.einsum('bhtd,bhde->bhte', qi * jnp.exp(bcum), state)
        b_last = bcum[:, :, -1:, :]
        k_dec = ki * jnp.exp(b_last - bcum)
        state = jnp.exp(b_last[:, :, 0, :])[..., None] * state \
            + jnp.einsum('bhsd,bhse->bhde', k_dec, vi)
        return state, o

    s0 = jnp.zeros((b, h, dk, dv), jnp.float32)
    _, o = lax.scan(step, s0, (qc, kc, vc, gc))
    return o.transpose(1, 2, 0, 3, 4).reshape(b, h, s, dv)

def hybrid_layer(x, layer, norm1_g, w_in, b_gate, lb_logits, hg_norm_g, w_o_sb, w_o_hg, w_out,
                 norm2_g, w_ff1, w_ff2):
    f32 = jnp.float32
    xn = rmsnorm(x, norm1_g[layer])
    u = xn @ w_in[layer].astype(f32)
    c = np.cumsum([SB_WIDTH, SB_WIDTH, SB_WIDTH, HG_WIDTH, HG_WIDTH, HG_WIDTH, HG_WIDTH, D_MODEL])
    q_sb, k_sb, v_sb, f_raw, i_hg, q_hg, g_hg, gate_sb, gate_hg = jnp.split(u, list(c), axis=-1)

    o_sb = stick_breaking_attention(split_heads(q_sb, SB_HEADS), split_heads(k_sb, SB_HEADS),
                                    split_heads(v_sb, SB_HEADS))
    o_sb = merge_heads(o_sb)

    lb_all = jnp.cumsum(jax.nn.softmax(lb_logits.astype(f32), axis=0), axis=0)
    lb = lb_all[layer]
    sig = jax.nn.sigmoid(f_raw)
    f = lb + (1.0 - lb) * sig
    log_f = jnp.log(f)
    k_hg = (1.0 - lb) * jax.nn.sigmoid(-f_raw)
    o_hg = hgrn2_chunkwise(split_heads(jax.nn.silu(q_hg), HG_HEADS), split_heads(k_hg, HG_HEADS),
                           split_heads(i_hg, HG_HEADS), split_heads(log_f, HG_HEADS))
    o_hg = rmsnorm(o_hg, hg_norm_g[layer].reshape(HG_HEADS, 1, HG_HEAD_DIM))
    o_hg = merge_heads(o_hg) * jax.nn.silu(g_hg)

    bg = b_gate[layer].astype(f32)
    g_a = jax.nn.sigmoid(gate_sb + bg[:D_MODEL])
    g_b = jax.nn.sigmoid(gate_hg + bg[D_MODEL:])
    merged = g_a * (o_sb @ w_o_sb[layer].astype(f32)) + g_b * (o_hg @ w_o_hg[layer].astype(f32))
    h = x.astype(f32) + merged @ w_out[layer].astype(f32)

    hn = rmsnorm(h, norm2_g[layer])
    a = jnp.square(jax.nn.relu(hn @ w_ff1[layer].astype(f32)))
    h = h + a @ w_ff2[layer].astype(f32)
    return h

def first_inputs(seed: int = 0) -> dict:
    key = jax.random.key(seed)
    ks = jax.random.split(key, 14)
    f32 = jnp.float32

    def nrm(k, shape, fan_in):
        return jax.random.normal(k, shape, f32) * (fan_in ** -0.5)

    return {
        "x": jax.random.normal(ks[0], (BATCH, SEQ, D_MODEL), f32),
        "norm1_g": 1.0 + 0.05 * jax.random.normal(ks[1], (DEPTH, D_MODEL), f32),
        "w_in": nrm(ks[2], (DEPTH, D_MODEL, IN_COLS), D_MODEL),
        "b_gate": 0.05 * jax.random.normal(ks[3], (DEPTH, N_BRANCH * D_MODEL), f32),
        "lb_logits": 0.5 * jax.random.normal(ks[4], (DEPTH + 1, HG_WIDTH), f32),
        "hg_norm_g": 1.0 + 0.05 * jax.random.normal(ks[5], (DEPTH, HG_WIDTH), f32),
        "w_o_sb": nrm(ks[6], (DEPTH, SB_WIDTH, D_MODEL), SB_WIDTH),
        "w_o_hg": nrm(ks[7], (DEPTH, HG_WIDTH, D_MODEL), HG_WIDTH),
        "w_out": nrm(ks[8], (DEPTH, D_MODEL, D_MODEL), D_MODEL),
        "norm2_g": 1.0 + 0.05 * jax.random.normal(ks[9], (DEPTH, D_MODEL), f32),
        "w_ff1": nrm(ks[10], (DEPTH, D_MODEL, D_FF), D_MODEL),
        "w_ff2": nrm(ks[11], (DEPTH, D_FF, D_MODEL), D_FF),
        "final_g": 1.0 + 0.05 * jax.random.normal(ks[12], (D_MODEL,), f32),
    }

def first_block(x, norm1_g, w_in, b_gate, lb_logits, hg_norm_g, w_o_sb, w_o_hg, w_out,
              norm2_g, w_ff1, w_ff2, final_g):
    h = x.astype(jnp.float32)
    for layer in range(DEPTH):
        h = hybrid_layer(h, layer, norm1_g, w_in, b_gate, lb_logits, hg_norm_g, w_o_sb, w_o_hg,
                         w_out, norm2_g, w_ff1, w_ff2)
    return rmsnorm(h, final_g).astype(x.dtype)


DEPTH_2 = 2

N_MIXERS = 4
N_PER_MIXER = tuple((DEPTH_2 - m + N_MIXERS - 1) // N_MIXERS for m in range(N_MIXERS))
PLE_DIM = 256
ROPE_THETA = 10000.0
D_FF_2 = (-((-8 * D_MODEL) // 3) + 255) // 256 * 256

GLA_HEADS = 4
GLA_DK = D_MODEL // 2
GLA_DV = D_MODEL
GLA_HK = GLA_DK // GLA_HEADS
GLA_HV = GLA_DV // GLA_HEADS
GLA_RANK = 16
GLA_TAU = 16.0
GLA_CHUNK = 64
GLA_IN = 2 * GLA_DK + 2 * GLA_DV + 2 * GLA_RANK

DIFF_HEAD_DIM = 64
DIFF_HEADS = D_MODEL // (2 * DIFF_HEAD_DIM)
DIFF_IN = 3 * D_MODEL

SSD_D_INNER = 2 * D_MODEL
SSD_HEAD_DIM = 64
SSD_HEADS = SSD_D_INNER // SSD_HEAD_DIM
SSD_GROUPS = 8
SSD_STATE = 128
SSD_CONV = 5
SSD_CHUNK = 128
SSD_CONV_DIM = SSD_D_INNER + 2 * SSD_GROUPS * SSD_STATE
SSD_IN = SSD_D_INNER + SSD_CONV_DIM + 2 * SSD_HEADS

DIL_PAIRS = ((128, 1), (512, 4), (2048, 16))
DIL_GROUPS = len(DIL_PAIRS)
DIL_HEADS = 16
DIL_HEAD_DIM = 64
DIL_WIDTH = DIL_HEADS * DIL_HEAD_DIM
DIL_IN = 3 * DIL_GROUPS * DIL_WIDTH


F32 = jnp.float32

def split_cols(x, sizes):
    out, start = [], 0
    for s in sizes:
        out.append(x[..., start:start + s])
        start += s
    return out

def rms_norm(x, g):
    xf = x.astype(F32)
    y = xf * lax.rsqrt(jnp.mean(xf * xf, axis=-1, keepdims=True) + EPS)
    return (y * g.astype(F32)).astype(x.dtype)

def rope(x, pos):
    hd = x.shape[-1]
    half = hd // 2
    inv = ROPE_THETA ** (-jnp.arange(half, dtype=F32) * 2.0 / hd)
    ang = pos.astype(F32)[:, None] * inv[None, :]
    cos = jnp.cos(ang)[:, None, :]
    sin = jnp.sin(ang)[:, None, :]
    xf = x.astype(F32)
    x1, x2 = xf[..., :half], xf[..., half:]
    return jnp.concatenate([x1 * cos - x2 * sin, x2 * cos + x1 * sin], axis=-1).astype(x.dtype)

def swiglu(h, w_in, w_out):
    g, u = split_cols(h @ w_in, [D_FF_2, D_FF_2])
    return (jax.nn.silu(g) * u) @ w_out

def gla_chunked(q, k, v, log_a, strict):
    bsz, nh, seq, dk = q.shape
    dv = v.shape[-1]
    c = GLA_CHUNK
    n = seq // c
    qf = q.astype(F32).reshape(bsz, nh, n, c, dk)
    kf = k.astype(F32).reshape(bsz, nh, n, c, dk)
    vf = v.astype(F32).reshape(bsz, nh, n, c, dv)
    b = jnp.cumsum(log_a.astype(F32).reshape(bsz, nh, n, c, dk), axis=3)
    b_last = b[:, :, :, -1:, :]
    q_in = qf * jnp.exp(b)
    scores = jnp.einsum('bhncd,bhnjd->bhncj', q_in, kf * jnp.exp(-b))
    mask = jnp.tril(jnp.ones((c, c), dtype=bool), -1 if strict else 0)
    scores = jnp.where(mask, scores, 0.0)
    o_intra = jnp.einsum('bhncj,bhnje->bhnce', scores, vf)
    u = jnp.einsum('bhncd,bhnce->bhnde', kf * jnp.exp(b_last - b), vf)
    decay = jnp.exp(b_last[:, :, :, 0, :])

    def step(s_prev, inp):
        u_n, a_n = inp
        return s_prev * a_n[..., None] + u_n, s_prev

    s0 = jnp.zeros((bsz, nh, dk, dv), F32)
    _, s_prev = lax.scan(step, s0, (jnp.moveaxis(u, 2, 0), jnp.moveaxis(decay, 2, 0)))
    s_prev = jnp.moveaxis(s_prev, 0, 2)
    o_inter = jnp.einsum('bhncd,bhnde->bhnce', q_in, s_prev)
    return (o_intra + o_inter).reshape(bsz, nh, seq, dv)

def gla_mixer(h, w_in, w_gate_f, b_gate_f, w_gate_b, b_gate_b, g_out, w_out):
    bsz, seq, _ = h.shape
    q, k, v, r, zf, zb = split_cols(h @ w_in, [GLA_DK, GLA_DK, GLA_DV, GLA_DV, GLA_RANK, GLA_RANK])

    def heads(t, hd):
        return t.reshape(bsz, seq, GLA_HEADS, hd).transpose(0, 2, 1, 3)

    qh = heads(q, GLA_HK) * (GLA_HK ** -0.5)
    kh = heads(k, GLA_HK)
    vh = heads(v, GLA_HV)
    la_f = heads(jax.nn.log_sigmoid((zf @ w_gate_f + b_gate_f).astype(F32)) / GLA_TAU, GLA_HK)
    la_b = heads(jax.nn.log_sigmoid((zb @ w_gate_b + b_gate_b).astype(F32)) / GLA_TAU, GLA_HK)

    def flip(t):
        return jnp.flip(t, axis=2)

    o = gla_chunked(qh, kh, vh, la_f, False) + flip(
        gla_chunked(flip(qh), flip(kh), flip(vh), flip(la_b), True))
    o = rms_norm(o.transpose(0, 2, 1, 3).astype(h.dtype), g_out).reshape(bsz, seq, GLA_DV)
    return (o * jax.nn.silu(r)) @ w_out

def diff_attn_mixer(h, pos, w_in, g_q, g_k, lam_q1, lam_k1, lam_q2, lam_k2, g_sub, w_out, lambda_init):
    bsz, seq, _ = h.shape
    nh, dh = DIFF_HEADS, DIFF_HEAD_DIM
    q, k, v = split_cols(h @ w_in, [D_MODEL, D_MODEL, D_MODEL])
    q = rms_norm(q.reshape(bsz, seq, nh, 2, dh), g_q)
    k = rms_norm(k.reshape(bsz, seq, nh, 2, dh), g_k)
    q = rope(q.reshape(bsz, seq, 2 * nh, dh), pos).reshape(bsz, seq, nh, 2, dh)
    k = rope(k.reshape(bsz, seq, 2 * nh, dh), pos).reshape(bsz, seq, nh, 2, dh)
    lam = (jnp.exp(jnp.sum(lam_q1.astype(F32) * lam_k1.astype(F32)))
           - jnp.exp(jnp.sum(lam_q2.astype(F32) * lam_k2.astype(F32))) + lambda_init)
    nb = seq // Q_BLOCK
    qb = q.reshape(bsz, nb, Q_BLOCK, nh, 2, dh).transpose(1, 0, 3, 4, 2, 5)
    kt = k.transpose(0, 2, 3, 1, 4)
    vt = v.reshape(bsz, seq, nh, 2 * dh).transpose(0, 2, 1, 3)
    scale = dh ** -0.5

    def block(q_blk):
        s = jnp.einsum('bhtqd,bhtkd->bhtqk', q_blk, kt).astype(F32) * scale
        pr = jax.nn.softmax(s, axis=-1)
        a = pr[:, :, 0] - lam * pr[:, :, 1]
        return jnp.einsum('bhqk,bhkd->bhqd', a.astype(vt.dtype), vt)

    o = lax.map(block, qb)
    o = o.transpose(1, 0, 3, 2, 4).reshape(bsz, seq, nh, 2 * dh)
    o = rms_norm(o, g_sub) * (1.0 - lambda_init)
    return o.reshape(bsz, seq, D_MODEL) @ w_out

def depthwise_conv_centered(x, w, b):
    width, ch = w.shape
    y = lax.conv_general_dilated(
        x, w[:, None, :].astype(x.dtype), window_strides=(1,),
        padding=[((width - 1) // 2, width // 2)],
        dimension_numbers=('NWC', 'WIO', 'NWC'), feature_group_count=ch)
    return y + b

def ssd_chunked(x, dt, a, bm, cm, strict):
    bsz, seq, nh, hp = x.shape
    ng, ns = bm.shape[2], bm.shape[3]
    hg = nh // ng
    c = SSD_CHUNK
    nc = seq // c
    xdt = (x.astype(F32) * dt[..., None]).reshape(bsz, nc, c, ng, hg, hp)
    acum = jnp.cumsum((dt * a).reshape(bsz, nc, c, ng, hg), axis=2)
    bc = bm.astype(F32).reshape(bsz, nc, c, ng, ns)
    cc = cm.astype(F32).reshape(bsz, nc, c, ng, ns)
    mask = jnp.tril(jnp.ones((c, c), dtype=bool), -1 if strict else 0)[:, :, None, None]
    diff = acum[:, :, :, None] - acum[:, :, None, :]
    lmat = jnp.where(mask, jnp.exp(jnp.where(mask, diff, 0.0)), 0.0)
    cb = jnp.einsum('bnigs,bnjgs->bnijg', cc, bc)
    y_diag = jnp.einsum('bnijg,bnijgh,bnjghp->bnighp', cb, lmat, xdt)
    a_last = acum[:, :, -1]
    decay_states = jnp.exp(a_last[:, :, None] - acum)
    states = jnp.einsum('bnjgs,bnjgh,bnjghp->bnghps', bc, decay_states, xdt)

    def step(s_prev, inp):
        st, dec = inp
        return s_prev * dec[..., None, None] + st, s_prev

    s0 = jnp.zeros((bsz, ng, hg, hp, ns), F32)
    _, prev = lax.scan(step, s0, (jnp.moveaxis(states, 1, 0), jnp.moveaxis(jnp.exp(a_last), 1, 0)))
    prev = jnp.moveaxis(prev, 0, 1)
    y_off = jnp.einsum('bnigs,bnigh,bnghps->bnighp', cc, jnp.exp(acum), prev)
    return (y_diag + y_off).reshape(bsz, seq, nh, hp)

def ssd_mixer(h, w_in, conv_w, conv_b, dt_bias_f, a_log_f, dt_bias_b, a_log_b, d_skip, g_norm, w_out):
    bsz, seq, _ = h.shape
    z, xbc, dt_f, dt_b = split_cols(h @ w_in, [SSD_D_INNER, SSD_CONV_DIM, SSD_HEADS, SSD_HEADS])
    xbc = jax.nn.silu(depthwise_conv_centered(xbc, conv_w, conv_b))
    xs, bm, cm = split_cols(xbc, [SSD_D_INNER, SSD_GROUPS * SSD_STATE, SSD_GROUPS * SSD_STATE])
    xs = xs.reshape(bsz, seq, SSD_HEADS, SSD_HEAD_DIM)
    bm = bm.reshape(bsz, seq, SSD_GROUPS, SSD_STATE)
    cm = cm.reshape(bsz, seq, SSD_GROUPS, SSD_STATE)
    dtf = jax.nn.softplus((dt_f + dt_bias_f).astype(F32))
    dtb = jax.nn.softplus((dt_b + dt_bias_b).astype(F32))
    af = -jnp.exp(a_log_f.astype(F32))
    ab = -jnp.exp(a_log_b.astype(F32))

    def flip(t):
        return jnp.flip(t, axis=1)

    y = ssd_chunked(xs, dtf, af, bm, cm, False) + flip(
        ssd_chunked(flip(xs), flip(dtb), ab, flip(bm), flip(cm), True))
    y = y + xs.astype(F32) * d_skip.astype(F32)[:, None]
    y = y.astype(h.dtype).reshape(bsz, seq, SSD_D_INNER) * jax.nn.silu(z)
    y = rms_norm(y.reshape(bsz, seq, SSD_GROUPS, SSD_D_INNER // SSD_GROUPS),
                 g_norm.reshape(SSD_GROUPS, SSD_D_INNER // SSD_GROUPS))
    return y.reshape(bsz, seq, SSD_D_INNER) @ w_out

def dilated_group(q, k, v, window, dilation):
    bsz, seq, nh, hd = q.shape
    n_side = (window // 2) // dilation
    offsets = dilation * jnp.arange(-n_side, n_side + 1, dtype=jnp.int32)
    nb = seq // Q_BLOCK
    qb = q.reshape(bsz, nb, Q_BLOCK, nh, hd).swapaxes(0, 1)
    starts = jnp.arange(nb, dtype=jnp.int32) * Q_BLOCK
    scale = hd ** -0.5

    def block(args):
        q_blk, start = args
        idx = (start + jnp.arange(Q_BLOCK, dtype=jnp.int32))[:, None] + offsets[None, :]
        valid = (idx >= 0) & (idx < seq)
        idx = jnp.clip(idx, 0, seq - 1)
        kg = k[:, idx]
        vg = v[:, idx]
        s = jnp.einsum('bqhd,bqmhd->bqhm', q_blk, kg).astype(F32) * scale
        s = jnp.where(valid[None, :, None, :], s, -jnp.inf)
        m = jnp.max(s, axis=-1, keepdims=True)
        e = jnp.exp(s - m)
        l = jnp.sum(e, axis=-1, keepdims=True)
        o = jnp.einsum('bqhm,bqmhd->bqhd', (e / l).astype(vg.dtype), vg)
        return o, (m + jnp.log(l))[..., 0]

    o, lse = lax.map(block, (qb, starts))
    return (o.swapaxes(0, 1).reshape(bsz, seq, nh, hd),
            lse.swapaxes(0, 1).reshape(bsz, seq, nh))

def dilated_mixer(h, pos, w_in, g_q, g_k, w_out):
    bsz, seq, _ = h.shape
    qkv = (h @ w_in).reshape(bsz, seq, 3, DIL_GROUPS, DIL_HEADS, DIL_HEAD_DIM)
    q = rms_norm(qkv[:, :, 0], g_q[:, None, :])
    k = rms_norm(qkv[:, :, 1], g_k[:, None, :])
    v = qkv[:, :, 2]
    flat = (bsz, seq, DIL_GROUPS * DIL_HEADS, DIL_HEAD_DIM)
    q = rope(q.reshape(flat), pos).reshape(bsz, seq, DIL_GROUPS, DIL_HEADS, DIL_HEAD_DIM)
    k = rope(k.reshape(flat), pos).reshape(bsz, seq, DIL_GROUPS, DIL_HEADS, DIL_HEAD_DIM)
    outs, lses = [], []
    for gi, (window, dilation) in enumerate(DIL_PAIRS):
        o, lse = dilated_group(q[:, :, gi], k[:, :, gi], v[:, :, gi], window, dilation)
        outs.append(o.astype(F32))
        lses.append(lse)
    wts = jax.nn.softmax(jnp.stack(lses, axis=0), axis=0)
    o = jnp.sum(wts[..., None] * jnp.stack(outs, axis=0), axis=0)
    return o.astype(h.dtype).reshape(bsz, seq, DIL_WIDTH) @ w_out

def second_inputs(seed: int = 0) -> dict:
    key = jax.random.key(seed)
    ks = iter(jax.random.split(key, 48))
    n_a, n_b, n_c, n_d = N_PER_MIXER

    def nrm(shape, std):
        return jax.random.normal(next(ks), shape, F32) * std

    def dense(shape):
        return nrm(shape, shape[-2] ** -0.5)

    def gain(shape):
        return 1.0 + nrm(shape, 0.05)

    x = nrm((BATCH, SEQ, D_MODEL), 1.0)
    p = nrm((DEPTH_2, BATCH, SEQ, PLE_DIM), 1.0)

    def dt_bias(shape):
        dt = jnp.exp(jax.random.uniform(next(ks), shape, F32, math.log(1e-3), math.log(1e-1)))
        return dt + jnp.log(-jnp.expm1(-dt))

    def a_log(shape):
        return jnp.log(jax.random.uniform(next(ks), shape, F32, 1.0, 16.0))

    return {
        'x': x,
        'p': p,
        'norm_mix': gain((DEPTH_2, D_MODEL)),
        'norm_ffn': gain((DEPTH_2, D_MODEL)),
        'ffn_w_in': dense((DEPTH_2, D_MODEL, 2 * D_FF_2)),
        'ffn_w_out': dense((DEPTH_2, D_FF_2, D_MODEL)),
        'ple_norm': gain((DEPTH_2, D_MODEL)),
        'ple_w_gate': dense((DEPTH_2, D_MODEL, D_MODEL)),
        'ple_w_proj': dense((DEPTH_2, PLE_DIM, D_MODEL)),
        'gla_w_in': dense((n_a, D_MODEL, GLA_IN)),
        'gla_w_gate_f': dense((n_a, GLA_RANK, GLA_DK)),
        'gla_b_gate_f': nrm((n_a, GLA_DK), 0.01),
        'gla_w_gate_b': dense((n_a, GLA_RANK, GLA_DK)),
        'gla_b_gate_b': nrm((n_a, GLA_DK), 0.01),
        'gla_g_out': gain((n_a, GLA_HV)),
        'gla_w_out': dense((n_a, GLA_DV, D_MODEL)),
        'diff_w_in': dense((n_b, D_MODEL, DIFF_IN)),
        'diff_g_q': gain((n_b, 2, DIFF_HEAD_DIM)),
        'diff_g_k': gain((n_b, 2, DIFF_HEAD_DIM)),
        'diff_lam_q1': nrm((n_b, DIFF_HEAD_DIM), 0.1),
        'diff_lam_k1': nrm((n_b, DIFF_HEAD_DIM), 0.1),
        'diff_lam_q2': nrm((n_b, DIFF_HEAD_DIM), 0.1),
        'diff_lam_k2': nrm((n_b, DIFF_HEAD_DIM), 0.1),
        'diff_g_sub': gain((n_b, 2 * DIFF_HEAD_DIM)),
        'diff_w_out': dense((n_b, D_MODEL, D_MODEL)),
        'ssd_w_in': dense((n_c, D_MODEL, SSD_IN)),
        'ssd_conv_w': nrm((n_c, SSD_CONV, SSD_CONV_DIM), SSD_CONV ** -0.5),
        'ssd_conv_b': nrm((n_c, SSD_CONV_DIM), 0.01),
        'ssd_dt_bias_f': dt_bias((n_c, SSD_HEADS)),
        'ssd_a_log_f': a_log((n_c, SSD_HEADS)),
        'ssd_dt_bias_b': dt_bias((n_c, SSD_HEADS)),
        'ssd_a_log_b': a_log((n_c, SSD_HEADS)),
        'ssd_d': gain((n_c, SSD_HEADS)),
        'ssd_g_norm': gain((n_c, SSD_D_INNER)),
        'ssd_w_out': dense((n_c, SSD_D_INNER, D_MODEL)),
        'dil_w_in': dense((n_d, D_MODEL, DIL_IN)),
        'dil_g_q': gain((n_d, DIL_GROUPS, DIL_HEAD_DIM)),
        'dil_g_k': gain((n_d, DIL_GROUPS, DIL_HEAD_DIM)),
        'dil_w_out': dense((n_d, DIL_WIDTH, D_MODEL)),
    }

def second_block(x, p, norm_mix, norm_ffn, ffn_w_in, ffn_w_out, ple_norm, ple_w_gate, ple_w_proj,
              gla_w_in, gla_w_gate_f, gla_b_gate_f, gla_w_gate_b, gla_b_gate_b, gla_g_out, gla_w_out,
              diff_w_in, diff_g_q, diff_g_k, diff_lam_q1, diff_lam_k1, diff_lam_q2, diff_lam_k2,
              diff_g_sub, diff_w_out,
              ssd_w_in, ssd_conv_w, ssd_conv_b, ssd_dt_bias_f, ssd_a_log_f, ssd_dt_bias_b,
              ssd_a_log_b, ssd_d, ssd_g_norm, ssd_w_out,
              dil_w_in, dil_g_q, dil_g_k, dil_w_out):
    seq = x.shape[1]
    pos = jnp.arange(seq, dtype=jnp.int32)
    h = x
    for i in range(DEPTH_2):
        kind = i % N_MIXERS
        j = i // N_MIXERS
        hn = rms_norm(h, norm_mix[i])
        if kind == 0:
            mix = gla_mixer(hn, gla_w_in[j], gla_w_gate_f[j], gla_b_gate_f[j], gla_w_gate_b[j],
                            gla_b_gate_b[j], gla_g_out[j], gla_w_out[j])
        elif kind == 1:
            lambda_init = 0.8 - 0.6 * math.exp(-0.3 * i)
            mix = diff_attn_mixer(hn, pos, diff_w_in[j], diff_g_q[j], diff_g_k[j], diff_lam_q1[j],
                                  diff_lam_k1[j], diff_lam_q2[j], diff_lam_k2[j], diff_g_sub[j],
                                  diff_w_out[j], lambda_init)
        elif kind == 2:
            mix = ssd_mixer(hn, ssd_w_in[j], ssd_conv_w[j], ssd_conv_b[j], ssd_dt_bias_f[j],
                            ssd_a_log_f[j], ssd_dt_bias_b[j], ssd_a_log_b[j], ssd_d[j],
                            ssd_g_norm[j], ssd_w_out[j])
        else:
            mix = dilated_mixer(hn, pos, dil_w_in[j], dil_g_q[j], dil_g_k[j], dil_w_out[j])
        h = h + mix
        h = h + swiglu(rms_norm(h, norm_ffn[i]), ffn_w_in[i], ffn_w_out[i])
        gate = jax.nn.sigmoid(rms_norm(h, ple_norm[i]) @ ple_w_gate[i])
        h = h + gate * (p[i] @ ple_w_proj[i])
    return h


def setup_inputs(seed=0):
    out = dict(first_inputs(seed))
    for name, value in second_inputs(seed + 1).items():
        if name != "x":
            out[name + "_2"] = value
    return out


def reference(
    x, norm1_g, w_in, b_gate, lb_logits, hg_norm_g, w_o_sb, w_o_hg, w_out, norm2_g, w_ff1,
    w_ff2, final_g, p_2, norm_mix_2, norm_ffn_2, ffn_w_in_2, ffn_w_out_2, ple_norm_2,
    ple_w_gate_2, ple_w_proj_2, gla_w_in_2, gla_w_gate_f_2, gla_b_gate_f_2, gla_w_gate_b_2,
    gla_b_gate_b_2, gla_g_out_2, gla_w_out_2, diff_w_in_2, diff_g_q_2, diff_g_k_2,
    diff_lam_q1_2, diff_lam_k1_2, diff_lam_q2_2, diff_lam_k2_2, diff_g_sub_2, diff_w_out_2,
    ssd_w_in_2, ssd_conv_w_2, ssd_conv_b_2, ssd_dt_bias_f_2, ssd_a_log_f_2, ssd_dt_bias_b_2,
    ssd_a_log_b_2, ssd_d_2, ssd_g_norm_2, ssd_w_out_2, dil_w_in_2, dil_g_q_2, dil_g_k_2,
    dil_w_out_2,
):
    x = first_block(
        x, norm1_g, w_in, b_gate, lb_logits, hg_norm_g, w_o_sb, w_o_hg, w_out, norm2_g, w_ff1,
        w_ff2, final_g,
    )
    return second_block(
        x, p_2, norm_mix_2, norm_ffn_2, ffn_w_in_2, ffn_w_out_2, ple_norm_2, ple_w_gate_2,
        ple_w_proj_2, gla_w_in_2, gla_w_gate_f_2, gla_b_gate_f_2, gla_w_gate_b_2,
        gla_b_gate_b_2, gla_g_out_2, gla_w_out_2, diff_w_in_2, diff_g_q_2, diff_g_k_2,
        diff_lam_q1_2, diff_lam_k1_2, diff_lam_q2_2, diff_lam_k2_2, diff_g_sub_2, diff_w_out_2,
        ssd_w_in_2, ssd_conv_w_2, ssd_conv_b_2, ssd_dt_bias_f_2, ssd_a_log_f_2, ssd_dt_bias_b_2,
        ssd_a_log_b_2, ssd_d_2, ssd_g_norm_2, ssd_w_out_2, dil_w_in_2, dil_g_q_2, dil_g_k_2,
        dil_w_out_2,
    )


_drawn_inputs = setup_inputs


def setup_inputs(seed=0):
    import zlib

    import numpy as np

    out = dict(_drawn_inputs(seed))
    spreads = {}
    factors = {'b_gate': 4.635,
     'ple_norm_2': 5.852,
     'gla_b_gate_f_2': 8.0,
     'gla_b_gate_b_2': 8.0,
     'diff_g_q_2': 4.905,
     'diff_g_k_2': 4.918,
     'diff_lam_q1_2': 3.622,
     'diff_lam_k1_2': 6.987,
     'diff_lam_k2_2': 7.626,
     'diff_g_sub_2': 2.911}
    for name, (base, spread) in spreads.items():
        noise = np.random.default_rng([zlib.crc32(name.encode()), seed]).standard_normal(out[name].shape)
        drawn = base * np.exp(spread * noise) if base else spread * noise
        out[name] = jnp.asarray(drawn.astype(out[name].dtype))
    for name, factor in factors.items():
        out[name] = (out[name] * factor).astype(out[name].dtype)
    return out
```

```python
import math
from contextlib import ExitStack

import numpy as np
import concourse.bass as bass
from concourse import mybir

F32 = mybir.dt.float32
F32R = mybir.dt.float32r
BF16 = mybir.dt.bfloat16
U32 = mybir.dt.uint32
ALU = mybir.AluOpType
ACT = mybir.ActivationFunctionType
AX = mybir.AxisListType.X

T = 256
D = 1024
EPS = 1e-6
LAMBDA_INIT = 0.8 - 0.6 * math.exp(-0.3)

NR = 3
NW = 3
LOOK = 2
SLOT = 2048


def constants():
    p = np.arange(128)
    s, t = p[:, None], p[None, :]
    parts = {}
    parts["ident"] = (s == t)
    parts["ntri"] = -(s >= t).astype(np.float32)
    parts["none"] = -np.ones((128, 128))
    parts["before"] = (s < t)
    parts["neg"] = np.where(s < t, 0.0, -1e30)
    for n in range(7):
        m = 1 << n
        parts[f"lev{n}"] = (s // (2 * m) == t // (2 * m)) & (s % (2 * m) < m) & (t % (2 * m) >= m)
    parts["after64"] = (s % 64) > np.arange(64)[None, :]
    pos = np.arange(256, dtype=np.float32)
    inv = np.float32(10000.0) ** (-np.arange(32, dtype=np.float32) * np.float32(2.0) / np.float32(64))
    ang = (pos[:, None] * inv[None, :]).astype(np.float32)
    parts["cos"] = np.cos(ang).reshape(2, 128, 32).transpose(1, 0, 2).reshape(128, 64)
    parts["sin"] = np.sin(ang).reshape(2, 128, 32).transpose(1, 0, 2).reshape(128, 64)
    at, cols, off = {}, [], 0
    for k, v in parts.items():
        v = np.asarray(v, np.float32)
        at[k] = (off, off + v.shape[1])
        off += v.shape[1]
        cols.append(v)
    return np.ascontiguousarray(np.concatenate(cols, 1)), at


SMALL = [("g1", 8), ("g2", 8), ("bg", 16), ("lb0", 4), ("lb1", 4),
         ("nm0", 8), ("nm1", 8), ("nf0", 8), ("nf1", 8), ("pn0", 8), ("pn1", 8),
         ("gbf", 4), ("gbb", 4), ("hgg", 512), ("gog", 256), ("gq", 128), ("gk", 128),
         ("gsub", 128), ("lq1", 64), ("lk1", 64), ("lq2", 64), ("lk2", 64)]


def small_at():
    at, off = {}, 0
    for k, n in SMALL:
        at[k] = (off, off + n)
        off += n
    return at, off


class Engine:

    def __init__(self, sem):
        self.sem, self.n, self.ops, self.seen = sem, 0, [], {}

    def wait(self, after):
        for tok in after:
            if tok is None:
                continue
            if isinstance(tok, list):
                self.wait(tok)
                continue
            sem, val = tok
            if self.seen.get(id(sem), 0) < val:
                self.seen[id(sem)] = val
                self.ops.append(lambda e, sem=sem, val=val: e.wait_ge(sem, val))

    def do(self, fn, *after, inc=True):
        self.wait(after)
        if not inc:
            self.ops.append(fn)
            return None
        self.n += 1
        self.ops.append(lambda e: fn(e).then_inc(self.sem, 1))
        return (self.sem, self.n)

    def dma(self, fn, sem, val, *after):
        self.wait(after)
        self.ops.append(lambda e: fn(e).then_inc(sem, 16))
        return (sem, val)

    def here(self):
        return (self.sem, self.n)


def program(nc, io, out, stage=4):
    plan = []
    with ExitStack() as ctx:
        hw = place(nc, ctx)
        emit(nc, hw, io, out, plan, None, stage)
        engines = emit(nc, hw, io, out, [], plan, stage)
        block = ctx.enter_context(nc.Block())

        @block.sync
        def _(e):
            for f in engines["SP"].ops:
                f(e)

        @block.scalar
        def _(e):
            for f in engines["ACT"].ops:
                f(e)

        @block.vector
        def _(e):
            for f in engines["DVE"].ops:
                f(e)

        @block.gpsimd
        def _(e):
            for f in engines["POOL"].ops:
                f(e)

        @block.tensor
        def _(e):
            for f in engines["PE"].ops:
                f(e)


def place(nc, ctx):
    def sb(name, shape, dt=F32):
        return ctx.enter_context(nc.sbuf_tensor(name, shape, dt))

    hw = {}
    nconst = constants()[0].shape[1]
    hw["CON"] = sb("CON", [128, nconst])
    hw["SML"] = sb("SML", [128, small_at()[1]])
    hw["IDB"] = sb("IDB", [128, 128], BF16)
    hw["NEGB"] = sb("NEGB", [128, 128], BF16)
    hw["SC"] = sb("SC", [128, 1000])
    hw["RAW"] = sb("RAW", [128, NR, SLOT])
    hw["WH"] = sb("WH", [128, NW, SLOT], F32R)
    hw["WL"] = sb("WL", [128, NW, SLOT], F32R)
    hw["XH"] = sb("XH", [128, 2048], F32R)
    hw["XL"] = sb("XL", [128, 2048], F32R)
    hw["OH"] = sb("OH", [128, 2048], F32R)
    hw["OL"] = sb("OL", [128, 2048], F32R)
    hw["H"] = sb("H", [128, 2048])
    hw["HS"] = sb("HS", [128, 2048])
    hw["AR"] = sb("AR", [128, 17792])
    hw["PS"] = ctx.enter_context(nc.psum_tensor("PS", [128, 8, 512], F32))
    for n in ("SP", "ACT", "DVE", "POOL", "PE"):
        hw["s" + n] = ctx.enter_context(nc.semaphore("s" + n))
    hw["raw"] = [ctx.enter_context(nc.semaphore(f"raw{i}")) for i in range(NR)]
    for n in ("con", "sml", "x", "wg", "fg", "p", "out"):
        hw["d_" + n] = ctx.enter_context(nc.semaphore("d_" + n))
    return hw


def emit(nc, hw, io, out, said, plan, stage):
    SP, AC, DV, PO, PE = (Engine(hw["s" + n]) for n in ("SP", "ACT", "DVE", "POOL", "PE"))
    RAW, WH, WL, PS, AR, SC = hw["RAW"], hw["WH"], hw["WL"], hw["PS"], hw["AR"], hw["SC"]
    con_at = constants()[1]
    sml_at = small_at()[0]

    def con(k, rows=slice(0, 128)):
        a, b = con_at[k]
        return hw["CON"][rows, a:b]

    def sml(k):
        a, b = sml_at[k]
        return hw["SML"][:, a:b]

    def ar(off, n, rows=slice(0, 128)):
        assert off + n <= 17792
        return AR[rows, off:off + n]

    used = [0]

    def fresh(n):
        used[0] += n
        assert used[0] <= 1000
        return SC[:, used[0] - n:used[0]]

    pf = [[] for _ in range(8)]

    def act(o, i, f, *after, **kw):
        return AC.do(lambda e: e.activation(o, i, f, **kw), *after)

    def tt(E, o, a, b, op, *after):
        return E.do(lambda e: e.tensor_tensor(o, a, b, op), *after)

    def ts(E, o, a, s1, s2, op0, op1, *after):
        if s2 is None:
            return E.do(lambda e: e.tensor_scalar(o, a, s1, None, op0), *after)
        return E.do(lambda e: e.tensor_scalar(o, a, s1, s2, op0, op1), *after)

    def stt(o, a, s, b, op0, op1, *after):
        return DV.do(lambda e: e.scalar_tensor_tensor(out=o, in0=a, scalar=s, in1=b, op0=op0, op1=op1), *after)

    def mm(o, l, r, start, stop, *after, inc=False, skip=False):
        return PE.do(lambda e: e.matmul(o, l, r, start=start, stop=stop, skip_group_check=skip),
                     *after, inc=inc)

    def mm3(o, s, m, start, stop, inc=False):
        mm(o, s[0], m[0], start, False)
        mm(o, s[0], m[1], False, False)
        return mm(o, s[1], m[0], False, stop, inc=inc)

    def tr(o, i, *after, inc=False, k=128):
        return PE.do(lambda e: e.transpose(o, i, con("ident", slice(0, k))[:, 0:k]), *after, inc=inc)

    st = {"next": 0, "prep": 0, "h": [], "l": [], "pe": []}

    def prep(c):
        name, k0, nk, n0, nn = plan[c]
        src = io[name][k0 * 128:(k0 + nk) * 128, n0:n0 + nn].rearrange("(k p) n -> p k n", p=128)
        r, w, n = c % NR, c % NW, nk * nn
        dst = RAW[:, r, 0:n].rearrange("p (k n) -> p k n", k=nk)
        free = [st["h"][c - NR], st["l"][c - NR]] if c >= NR else []
        got = SP.dma(lambda e: e.dma_start(dst, src), hw["raw"][r], 16 * (c // NR + 1), free)
        idle = [st["pe"][c - NW]] if c >= NW else []
        wh, wl, raw = WH[:, w, 0:n], WL[:, w, 0:n], RAW[:, r, 0:n]
        h = act(wh, raw, ACT.Copy, got, idle)
        st["h"].append(h)
        st["l"].append(tt(DV, wl, raw, wh.bitcast(F32), ALU.subtract, got, h, idle))

    def take(name, k0, nk, n0, nn):
        c = st["next"]
        st["next"] += 1
        said.append((name, k0, nk, n0, nn))
        w = c % NW
        if plan is not None:
            while st["prep"] < min(c + LOOK + 1, len(plan)):
                prep(st["prep"])
                st["prep"] += 1
            PE.wait([st["h"][c], st["l"][c]])
        view = [x[:, w, 0:nk * nn].rearrange("p (k n) -> p k n", k=nk) for x in (WH, WL)]
        return view

    def done(tok):
        st["pe"].append(tok)

    def pair(n, kt=8, base=0):
        return tuple(hw[n + s][:, base:base + kt * 256].rearrange("p (k t) -> p k t", k=kt) for s in "HL")

    X = pair("X")
    O = pair("O")

    def feat(name, n0, bank, ops, *after):
        w = take(name, 0, 8, n0, 256)
        PE.wait([*after, pf[bank]])
        for fb in range(2):
            for k in range(8):
                tok = mm3(PS[:, bank, fb * 256:fb * 256 + 256],
                          [x[:, k, fb * 128:fb * 128 + 128] for x in w], [x[:, k, :] for x in ops],
                          k == 0, k == 7, inc=(fb == 1 and k == 7))
        done(tok)
        return tok

    def toks(name, n0, bank, ops, *after, nn=256):
        w = take(name, 0, 8, n0, nn)
        PE.wait([*after, pf[bank]])
        for tb in range(2):
            for k in range(8):
                tok = mm3(PS[:, bank, tb * nn:tb * nn + nn],
                          [x[:, k, tb * 128:tb * 128 + 128] for x in ops], [x[:, k, :] for x in w],
                          k == 0, k == 7, inc=(tb == 1 and k == 7))
        done(tok)
        return tok

    def down(name, kt, ops, ok, banks, first, last, *after):
        w = take(name, kt, 2, 0, 1024)
        PE.wait([*after])
        if first:
            PE.wait([pf[b] for b in banks])
        for k in range(2):
            for tb in range(2):
                for n in range(2):
                    end = k == 1 and tb == 1 and n == 1
                    tok = mm3(PS[:, banks[2 * tb + n], :],
                              [x[:, ok + k, tb * 128:tb * 128 + 128] for x in ops],
                              [x[:, k, n * 512:n * 512 + 512] for x in w],
                              first and k == 0, last and k == 1, inc=end)
        done(tok)
        return tok

    d_con = SP.dma(lambda e: e.dma_start(hw["CON"][:, :], io["const"]), hw["d_con"], 16)
    H = hw["H"][:, :].rearrange("p (b d) -> p b d", b=2)
    HS = hw["HS"][:, :].rearrange("p (b d) -> p b d", b=2)
    d_x = SP.dma(lambda e: e.dma_start(H, io["x"].rearrange("(b p) d -> p b d", p=128)), hw["d_x"], 16)
    d_sml = SP.dma(lambda e: e.dma_start(hw["SML"][:, :], io["small"]), hw["d_sml"], 16)
    SP.wait([])
    for E in (AC, DV, PO, PE):
        E.wait([d_con, d_sml])
    c1 = DV.do(lambda e: e.tensor_copy(hw["IDB"][:, :], con("ident")))
    c2 = DV.do(lambda e: e.tensor_copy(hw["NEGB"][:, :], con("neg")))
    PE.wait([c1, c2])

    def rstd(ss, n, inv, *after):
        ms, y, t = fresh(n), fresh(n), fresh(n)
        a = ts(DV, ms, ss, inv, EPS, ALU.mult, ALU.add, *after)
        a = act(y, ms, ACT.Ln, a)
        a = act(y, y, ACT.Exp, a, scale=-0.5)
        a = tt(DV, t, y, y, ALU.mult, a)
        a = stt(t, t, -0.5, ms, ALU.mult, ALU.mult, a)
        r = fresh(n)
        return r, stt(r, t, 1.5, y, ALU.add, ALU.mult, a)

    def rows_rstd(src, junk, *after):
        ss = fresh(2)
        for tb in range(2):
            a = act(junk[:, tb, :], src[:, tb, :], ACT.Square, *after, accum_out=ss[:, tb:tb + 1])
        return rstd(ss, 2, 1.0 / D, a)

    def split_evac(bank, n, hi, lo, g, *after):
        src = PS[:, bank, 0:n]
        a = act(hi, src, ACT.Copy, *after, **({} if g is None else {"scale": g}))
        if g is None:
            b = tt(DV, lo, src, hi.bitcast(F32), ALU.subtract, a)
        else:
            b = stt(lo, src, g, hi.bitcast(F32), ALU.mult, ALU.subtract, a)
        pf[bank] = [a, b]
        return [a, b]

    def turn(src, nk, dst, gains, banks, free, *after):
        toks_ = []
        for k in range(nk):
            bank = banks[k % len(banks)]
            PE.wait([*after, pf[bank]])
            tr(PS[:, bank, 0:128], src[:, 0, k * 128:k * 128 + 128])
            a = tr(PS[:, bank, 128:256], src[:, 1, k * 128:k * 128 + 128], inc=True)
            g = None if gains is None else gains[:, k:k + 1]
            toks_ += split_evac(bank, 256, dst[0][:, k, :], dst[1][:, k, :], g, a, free)
        return toks_[-2:]

    def norm_turn(hdep, gains, xfree, banks=range(4)):
        r, a = rows_rstd(H, HS, hdep)
        t = [ts(DV, HS[:, tb, :], H[:, tb, :], r[:, tb:tb + 1], None, ALU.mult, None, a) for tb in range(2)]
        return turn(HS, 8, X, gains, list(banks), xfree, t)

    v3 = lambda ap, a: ap.rearrange("p (a b) -> p a b", a=a)

    xt = norm_turn(d_x, sml("g1"), [])

    qT, kT, v = (ar(o, 1024) for o in (0, 1024, 2048))
    evs = []
    n = 0
    for sec, dst in ((0, qT), (512, kT), (1024, v)):
        for i in range(2):
            b = n % 2
            if sec < 1024:
                a = feat("w_in", sec + 256 * i, b, X, xt)
                o = v3(dst, 4)[:, 2 * i:2 * i + 2, :]
                s = v3(PS[:, b, :], 2)
            else:
                a = toks("w_in", sec + 256 * i, b, X, xt)
                o = v3(dst, 2)[:, :, 256 * i:256 * i + 256]
                s = v3(PS[:, b, :], 2)
            e = act(o, s, ACT.Copy, a, scale=0.125 if sec == 0 else 1.0)
            pf[b] = [e]
            evs.append(e)
            n += 1
    qkv = evs[-1]

    lf, bb, kh, qh, vh, GS = (ar(o, 1024) for o in (8576, 9600, 6528, 7552, 10624, 11648))
    tmp = ar(12672, 1024)
    tmp2 = ar(13696, 1024)

    lb, oml, w8 = fresh(4), fresh(4), fresh(12)
    a = tt(DV, w8[:, 0:4], sml("lb0"), sml("lb1"), ALU.max)
    a1 = tt(DV, w8[:, 4:8], sml("lb0"), w8[:, 0:4], ALU.subtract, a)
    a2 = tt(DV, w8[:, 8:12], sml("lb1"), w8[:, 0:4], ALU.subtract, a)
    a = act(w8[:, 4:12], w8[:, 4:12], ACT.Exp, a1, a2)
    a = tt(DV, w8[:, 0:4], w8[:, 4:8], w8[:, 8:12], ALU.add, a)
    a = DV.do(lambda e: e.reciprocal(w8[:, 0:4], w8[:, 0:4]), a)
    a = tt(DV, lb, w8[:, 4:8], w8[:, 0:4], ALU.mult, a)
    lbt = ts(DV, oml, lb, -1.0, 1.0, ALU.mult, ALU.add, a)

    hg = {}

    def fill_hg():
        k = 0
        ft = []
        for i in range(2):
            b = k % 2
            k += 1
            a = feat("w_in", 1536 + 256 * i, b, X)
            s = v3(PS[:, b, :], 2)
            sg = v3(tmp, 4)[:, 2 * i:2 * i + 2, :]
            ng = v3(tmp2, 4)[:, 2 * i:2 * i + 2, :]
            a1 = act(sg, s, ACT.Sigmoid, a)
            a2 = act(ng, s, ACT.Sigmoid, a, scale=-1.0)
            pf[b] = [a2]
            for j in range(2):
                h = 2 * i + j
                f1 = ts(DV, v3(lf, 4)[:, h, :], sg[:, j, :], oml[:, h:h + 1], lb[:, h:h + 1],
                        ALU.mult, ALU.add, a1, lbt)
                f2 = ts(DV, v3(kh, 4)[:, h, :], ng[:, j, :], oml[:, h:h + 1], None, ALU.mult, None, a2)
                ft += [f1, f2]
            yield
        for i in range(2):
            b = k % 2
            k += 1
            a = toks("w_in", 2048 + 256 * i, b, X)
            vt = act(v3(vh, 2)[:, :, 256 * i:256 * i + 256], v3(PS[:, b, :], 2), ACT.Copy, a)
            pf[b] = [vt]
            yield
        for i in range(2):
            b = k % 2
            k += 1
            a = feat("w_in", 2560 + 256 * i, b, X)
            qt = act(v3(qh, 4)[:, 2 * i:2 * i + 2, :], v3(PS[:, b, :], 2), ACT.Silu, a)
            pf[b] = [qt]
            yield
        for i in range(2):
            b = k % 2
            k += 1
            a = toks("w_in", 3072 + 256 * i, b, X)
            o = v3(GS, 2)[:, :, 256 * i:256 * i + 256]
            g1 = act(o, v3(PS[:, b, :], 2), ACT.Silu, a)
            pf[b] = [g1]
            gb = sml("hgg")[:, 256 * i:256 * i + 256].unsqueeze(1).to_broadcast([128, 2, 256])
            gt = tt(DV, o, o, gb, ALU.mult, g1)
            yield
        hg.update(f=ft[-1], v=vt, q=qt, g=gt)

    def drain(g):
        for _ in g:
            pass

    def stick(fill):
        V = v3(v, 2)
        work = lambda i, j: ar(3072 + 1152 * (i % 3) + 384 * j, 384)
        t0, t1, t2, wf = {}, {}, {}, {}
        osb = (hw["OH"][:, 0:1024], hw["OL"][:, 0:1024])
        res = []

        def A(h):
            j, base, z = h // 2, 64 * (h % 2), 2 + h % 3
            q = v3(qT, 4)[base:base + 64, j, :]
            k = v3(kT, 4)[base:base + 64, j, :]
            mm(PS[:, z, 0:256], k[:, 0:128], q, True, True, qkv, pf[z])
            a = mm(PS[:, z, 256:384], k[:, 128:256], q[:, 128:256], False, True, inc=True, skip=True)
            e, sp = work(h, 0), work(h, 1)
            Z = PS[:, z, 0:384]
            a1 = act(e, Z, ACT.Abs, a, wf.get(h - 3))
            a1 = act(e, e, ACT.Exp, a1, scale=-1.0)
            a1 = act(e, e, ACT.Ln, a1, bias=1.0)
            a2 = stt(sp, Z, 0.0, e, ALU.max, ALU.add, a1, t1.get(h - 3))
            dg = sp[:, 0:384].rearrange("p (a b) -> p a b", a=3)[:, 0:3:2, :]
            mk = con("before").unsqueeze(1).to_broadcast([128, 2, 128])
            t0[h] = tt(DV, dg, dg, mk, ALU.mult, a2)

        def B(h):
            z = 2 + h % 3
            sp, w = work(h, 1), work(h, 2)
            mm(PS[:, z, 0:384], con("ntri"), sp, False, True, t0[h], skip=True)
            mm(PS[:, z, 128:256], con("none"), sp[:, 256:384], False, True, skip=True)
            mm(PS[:, z, 0:128], hw["IDB"][:, :], hw["NEGB"][:, :], False, True, skip=True)
            t1[h] = mm(PS[:, z, 256:384], hw["IDB"][:, :], hw["NEGB"][:, :], False, True, inc=True, skip=True)
            t2[h] = act(w, PS[:, z, 0:384], ACT.Exp, t1[h], wf.get(h - 3))
            pf[z] = [t2[h]]

        def C(h):
            j, base, ob = h // 2, 64 * (h % 2), 5 + (h // 2) % 2
            w = work(h, 2)
            o = PS[base:base + 64, ob, 0:256]
            if h % 2 == 0:
                PE.wait(pf[ob])
            mm(o, V[:, 0, h * 64:h * 64 + 64], w[:, 0:256], True, True, t2[h])
            wf[h] = mm(PS[base:base + 64, ob, 128:256], V[:, 1, h * 64:h * 64 + 64], w[:, 256:384],
                       False, True, inc=True, skip=True)
            if h % 2 == 1:
                hi, lo = (x[:, j * 256:j * 256 + 256] for x in osb)
                res[:] = split_evac(ob, 256, hi, lo, None, wf[h])

        for i in range(10):
            if i < 8:
                A(i)
            if 1 <= i < 9:
                B(i - 1)
            if i >= 2:
                C(i - 2)
            next(fill, None)
        drain(fill)
        return res

    osb_t = stick(fill_hg())

    one128 = ar(13696, 1024)
    a = act(lf, lf, ACT.Ln, hg["f"])
    a1 = PO.do(lambda e: e.memset(one128, 1.0), hg["f"])
    a1 = PO.do(lambda e: e.memset(v3(one128, 8)[:, :, 0:1], 0.0), a1)
    bt = DV.do(lambda e: e.tensor_tensor_scan(bb, one128, lf, 0.0, ALU.mult, ALU.add), a, a1)

    ga = ar(0, 2048)
    gb_ = ar(2048, 2048)
    gates = {}

    def fill_gates():
        for i in range(8):
            b = i % 2
            a = feat("w_in", 3584 + 256 * i, b, X, PE.here() if False else None)
            dst = (ga if i < 4 else gb_)
            e = None
            for j in range(2):
                blk = 2 * (i % 4) + j
                e = act(v3(dst, 8)[:, blk, :], PS[:, b, 256 * j:256 * j + 256], ACT.Sigmoid, a, osb_t,
                        bias=sml("bg")[:, 2 * i + j:2 * i + j + 1])
            pf[b] = [e]
            yield
        gates["t"] = e

    def hgrn(fill):
        E_ = [ar(12672, 1024), ar(13696, 1024)]
        P_ = [ar(14720, 1024), ar(15744, 1024)]
        ACC = ar(16768, 1024)
        ACC2 = ar(8576, 512)
        A8 = v3(ACC, 8)
        for j in range(8):
            a = mm(PS[:, 2 + j // 4, 128 * (j % 4):128 * (j % 4) + 128], v3(kh, 8)[:, j, :],
                   v3(qh, 8)[:, j, :], True, True, hg["q"], hg["f"], pf[2], pf[3], inc=(j == 7))
        idb = con("ident").unsqueeze(1).to_broadcast([128, 8, 128])
        src = PS[:, 2:4, :].rearrange("p a (b c) -> p (a b) c", c=128)
        acc = tt(DV, A8, src, idb, ALU.mult, a)
        pf[2] = [acc]
        pf[3] = [acc]
        et, ptk = {}, {}
        for lv in range(7):
            m = 1 << lv
            E, P = E_[lv % 2], P_[lv % 2]
            cut = lambda ap: ap.rearrange("p (n m) -> p n m", m=2 * m)
            B = cut(bb)
            first, second = slice(0, m), slice(m, 2 * m)
            nb = 1024 // (2 * m)
            ref = B[:, :, m - 1:m].to_broadcast([128, nb, m])
            prev = [ptk.get(lv - 2)]
            a1 = tt(DV, cut(E)[:, :, second], B[:, :, second], ref, ALU.subtract, bt, prev)
            a2 = tt(DV, cut(E)[:, :, first], ref, B[:, :, first], ALU.subtract, prev)
            a = act(E, E, ACT.Exp, a1, a2)
            e1 = tt(PO, cut(P)[:, :, second], cut(E)[:, :, second], cut(qh)[:, :, second], ALU.mult, a, et.get(lv - 2))
            e2 = tt(DV, cut(P)[:, :, first], cut(E)[:, :, first], cut(kh)[:, :, first], ALU.mult, a, et.get(lv - 2))
            ptk[lv] = [e1, e2]
            p0 = 4 if lv % 2 == 0 else 2
            for j in range(8):
                a = mm(PS[:, p0 + j // 4, 128 * (j % 4):128 * (j % 4) + 128], v3(P, 8)[:, j, :],
                       v3(P, 8)[:, j, :], True, True, e1, e2, pf[p0], pf[p0 + 1], inc=(j == 7))
            et[lv] = a
            src = PS[:, p0:p0 + 2, :].rearrange("p a (b c) -> p (a b) c", c=128)
            mk = con(f"lev{lv}").bitcast(U32).unsqueeze(1).to_broadcast([128, 8, 128])
            acc = DV.do(lambda e, mk=mk, src=src: e.copy_predicated(A8, mk, src), a, acc)
            pf[p0] = [acc]
            pf[p0 + 1] = [acc]
            next(fill, None)
        E, P = E_[1], P_[1]
        B = v3(bb, 4)
        prev = ptk[5]
        a1 = tt(DV, v3(E, 4)[:, :, 0:128], B[:, :, 127:128].to_broadcast([128, 4, 128]), B[:, :, 0:128],
                ALU.subtract, prev)
        a2 = act(v3(E, 4)[:, :, 128:256], B[:, :, 128:256], ACT.Exp, bt, prev)
        a1 = act(v3(E, 4)[:, :, 0:128], v3(E, 4)[:, :, 0:128], ACT.Exp, a1)
        e1 = tt(PO, v3(P, 4)[:, :, 0:128], v3(E, 4)[:, :, 0:128], v3(kh, 4)[:, :, 0:128], ALU.mult, a1, et[5])
        e2 = tt(DV, v3(P, 4)[:, :, 128:256], v3(E, 4)[:, :, 128:256], v3(qh, 4)[:, :, 128:256], ALU.mult, a2, et[5])
        for h in range(4):
            a = mm(PS[:, 6, 128 * h:128 * h + 128], v3(P, 4)[:, h, 0:128], v3(P, 4)[:, h, 128:256],
                   True, True, e1, e2, pf[6], inc=(h == 3))
        a2 = act(ACC2, PS[:, 6, :], ACT.Copy, a, bt)
        pf[6] = [a2]
        V = v3(vh, 2)
        for tb in range(2):
            PE.wait([acc, a2, hg["v"], pf[4 + tb]])
            for h in range(4):
                o = PS[:, 4 + tb, 128 * h:128 * h + 128]
                a = mm(o, A8[:, 2 * h + tb, :], V[:, tb, 128 * h:128 * h + 128], True, tb == 0, inc=(h == 3 and tb == 0))
                if tb == 1:
                    a = mm(o, v3(ACC2, 4)[:, h, :], V[:, 0, 128 * h:128 * h + 128], False, True, inc=(h == 3))
            if tb == 0:
                o0 = a
        next(fill, None)
        sq = HS
        ss = fresh(8)
        a1 = act(sq[:, 0, 0:512], PS[:, 4, :], ACT.Square, o0)
        a2 = act(sq[:, 1, 0:512], PS[:, 5, :], ACT.Square, a)
        for tb in range(2):
            a3 = DV.do(lambda e, tb=tb: e.tensor_reduce(ss[:, 4 * tb:4 * tb + 4], v3(sq[:, tb, 0:512], 4), AX, ALU.add),
                       [a1, a2][tb])
        r, a = rstd(ss, 8, 1.0 / 128, a3)
        ot = []
        for tb in range(2):
            o = sq[:, tb, 512:1024]
            b = tt(DV, v3(o, 4), v3(PS[:, 4 + tb, :], 4), r[:, 4 * tb:4 * tb + 4].unsqueeze(2).to_broadcast([128, 4, 128]),
                   ALU.mult, a)
            pf[4 + tb] = [b]
            ot.append(tt(DV, o, o, v3(GS, 2)[:, tb, :], ALU.mult, b, hg["g"]))
        dst = pair("O", 4, 1024)
        return turn(sq[:, :, 512:1024], 4, dst, None, [2, 3, 6, 7], [], ot), fill

    ohg_t, fill = hgrn(fill_gates())
    drain(fill)

    if stage == 0:
        t = [tt(DV, hw["H"][:, :], hw["OH"][:, :].bitcast(F32), hw["OL"][:, :].bitcast(F32), ALU.add, osb_t, ohg_t)]
        e = SP.dma(lambda e: e.dma_start(out.rearrange("(b p) d -> p b d", p=128), H), hw["d_out"], 16, t)
        SP.wait([e])
        return {"SP": SP, "ACT": AC, "DVE": DV, "POOL": PO, "PE": PE}

    OS, OG = pair("O", 4, 0), pair("O", 4, 1024)
    mg = ar(4096, 2048)
    xin = PE.here()
    mt = []
    for c in range(2):
        halves = []
        for name, ops, b0, dep in (("w_o_sb", OS, 0, osb_t), ("w_o_hg", OG, 2, ohg_t)):
            b0 = b0 + 4 * c
            w = take(name, 0, 4, 512 * c, 512)
            PE.wait([dep, pf[b0], pf[b0 + 1]])
            for fb in range(4):
                for k in range(4):
                    a = mm3(PS[:, b0 + fb // 2, 256 * (fb % 2):256 * (fb % 2) + 256],
                            [x[:, k, fb * 128:fb * 128 + 128] for x in w], [x[:, k, :] for x in ops],
                            k == 0, k == 3, inc=(fb == 3 and k == 3))
            done(a)
            halves.append((b0, a))
        (ba, aa), (bg2, ag) = halves
        for i in range(2):
            g1 = ga[:, 1024 * c + 512 * i:1024 * c + 512 * i + 512]
            g2 = gb_[:, 1024 * c + 512 * i:1024 * c + 512 * i + 512]
            o = mg[:, 1024 * c + 512 * i:1024 * c + 512 * i + 512]
            a1 = tt(DV, g1, g1, PS[:, ba + i, :], ALU.mult, aa, gates["t"])
            a2 = tt(DV, g2, g2, PS[:, bg2 + i, :], ALU.mult, ag)
            pf[ba + i] = [a1]
            pf[bg2 + i] = [a2]
            a = tt(DV, o, g1, g2, ALU.add, a1, a2)
            hi, lo = (hw["X" + s][:, 1024 * c + 512 * i:1024 * c + 512 * i + 512] for s in "HL")
            b = act(hi, o, ACT.Copy, a, xin)
            mt += [b, tt(DV, lo, o, hi.bitcast(F32), ALU.subtract, b)]

    def residual(banks, a):
        t = []
        for tb in range(2):
            for n in range(2):
                b = banks[2 * tb + n]
                o = H[:, tb, 512 * n:512 * n + 512]
                e = tt(DV, o, o, PS[:, b, :], ALU.add, a)
                pf[b] = [e]
                t.append(e)
        return t

    def project(name, ops, dep, banks):
        for i in range(4):
            a = down(name, 2 * i, ops, 2 * i, banks, i == 0, i == 3, dep)
        return residual(banks, a)

    ht = project("w_out", X, mt, [0, 1, 2, 3])
    xfree = PE.here()

    xt = norm_turn(ht, sml("g2"), xfree, range(4, 8))

    def ffn(n, up, dname, xdep, name):
        ready = {}
        of = {}
        for i in range(n + 1):
            if i < n:
                ready[i] = up(i, of.get(i - 2))
            if i >= 1:
                j = i - 1
                s = j % 2
                ops = tuple(v3(x, 8)[:, 2 * s:2 * s + 2, :] for x in (hw["OH"][:, :], hw["OL"][:, :]))
                of[j] = down(dname, 2 * j, ops, 0, [4, 5, 6, 7], j == 0, j == n - 1, ready[j])
        return residual([4, 5, 6, 7], of[n - 1])

    def halves(i):
        s = i % 2
        return tuple(hw["O" + x][:, 512 * s:512 * s + 512] for x in "HL")

    def up_relu(i, of):
        b = i % 4
        a = feat("w_ff1", 256 * i, b, X, xt)
        w = ar(512 * (i % 2), 512)
        a = ts(DV, w, PS[:, b, :], 0.0, None, ALU.max, None, a)
        pf[b] = [a]
        a = act(w, w, ACT.Square, a)
        hi, lo = halves(i)
        b1 = act(hi, w, ACT.Copy, a, of)
        b2 = tt(DV, lo, w, hi.bitcast(F32), ALU.subtract, b1)
        return [b1, b2]

    DV.wait([PE.here(), AC.here()])
    ht = ffn(16, up_relu, "w_ff2", xt, "w_ff1")
    fg = ar(2048, 1024)
    d_fg = SP.dma(lambda e: e.dma_start(fg, io["final"]), hw["d_fg"], 16, xin)
    r, a = rows_rstd(H, HS, ht)
    ht = []
    for tb in range(2):
        ht.append(stt(H[:, tb, :], H[:, tb, :], r[:, tb:tb + 1], fg, ALU.mult, ALU.mult, a, d_fg))

    xfree = PE.here()
    dwg = SP.dma(lambda e: e.dma_start(ar(16768, 1024, slice(0, 16)), io["wgate"]), hw["d_wg"], 16, xin)

    def gla():
        xt = norm_turn(ht, sml("nm0"), xfree)
        F = [PE.here(), DV.here(), AC.here(), PO.here()]
        q, k = ar(0, 1024), ar(1024, 1024)
        v, r = ar(2048, 2048), ar(4096, 2048)
        AC.wait(F)
        DV.wait(F)
        PO.wait(F)
        b = 2
        a = toks("gla_w_in", 3072, b, X, xt, nn=32)
        z = ar(6144, 64)
        a = act(z, PS[:, b, 0:64], ACT.Copy, a)
        pf[b] = [a]
        z4 = z.rearrange("p (t d r) -> p t d r", t=2, d=2)
        zT = ar(6208, 512, slice(0, 16))
        PE.wait([a, pf[3]])
        for d in range(2):
            for tb in range(2):
                a = tr(PS[0:16, 3, 256 * d + 128 * tb:256 * d + 128 * tb + 128], z4[:, tb, d, :], inc=(d == 1 and tb == 1))
        zt = act(zT, PS[0:16, 3, :], ACT.Copy, a)
        pf[3] = [zt]
        wg = ar(16768, 1024, slice(0, 16)).rearrange("p (d n) -> p d n", d=2)
        L = [ar(6720, 1024), ar(7744, 1024)]
        M = [ar(8768, 1024), ar(9792, 1024)]
        ls = []
        for d in range(2):
            bs = [4, 5] if d == 0 else [6, 7]
            PE.wait([zt, dwg, pf[bs[0]], pf[bs[1]]])
            for h in range(4):
                a = mm(PS[:, bs[h // 2], 256 * (h % 2):256 * (h % 2) + 256], wg[:, d, 128 * h:128 * h + 128],
                       zT[:, 256 * d:256 * d + 256], True, True, inc=(h == 3))
            for h in range(4):
                src = PS[:, bs[h // 2], 256 * (h % 2):256 * (h % 2) + 256]
                bias = sml("gbf" if d == 0 else "gbb")[:, h:h + 1]
                e2 = ts(DV, M[d][:, 256 * h:256 * h + 256], src, bias, None, ALU.add, None, a)
            pf[bs[0]] = [e2]
            pf[bs[1]] = [e2]
            e1 = act(L[d], M[d], ACT.Abs, e2)
            e1 = act(L[d], L[d], ACT.Exp, e1, scale=-1.0)
            e1 = act(L[d], L[d], ACT.Ln, e1, bias=1.0)
            ls.append(stt(M[d], M[d], 0.0, L[d], ALU.min, ALU.subtract, e1))
        one64 = ar(10816, 1024)
        a1 = PO.do(lambda e: e.memset(one64, 1.0))
        a1 = PO.do(lambda e: e.memset(v3(one64, 16)[:, :, 0:1], 0.0), a1)
        bf, bp = L
        s1 = DV.do(lambda e: e.tensor_tensor_scan(bf, one64, M[0], 0.0, ALU.mult, ALU.add), ls[0], a1)
        s2 = DV.do(lambda e: e.tensor_tensor_scan(bp, one64, M[1], 0.0, ALU.mult, ALU.add), ls[1])
        c16 = lambda ap: v3(ap, 16)
        tot = lambda ap: c16(ap)[:, :, 63:64].to_broadcast([128, 16, 64])
        totf, totb = fresh(16), fresh(16)
        x1 = act(totf, bf.rearrange("p (c j) -> p c j", c=16)[:, :, 63:64].rearrange("p c j -> p (c j)"),
                 ACT.Exp, s1, scale=1 / 16)
        x2 = act(totb, bp.rearrange("p (c j) -> p c j", c=16)[:, :, 63:64].rearrange("p c j -> p (c j)"),
                 ACT.Exp, s2, scale=1 / 16)
        fq, fk, fd = ar(11840, 1024), ar(12864, 1024), ar(13888, 1024)
        df = tt(DV, c16(fd), tot(bf), c16(bf), ALU.subtract, s1)
        bd_ = M[1]
        db = tt(DV, bd_, bp, M[1], ALU.subtract, s2)
        bq = ar(14912, 1024)
        dc = tt(DV, c16(bq), tot(bp), c16(bd_), ALU.subtract, db)
        y = {}
        y["fq"] = act(fq, bf, ACT.Exp, s1, scale=1 / 16)
        y["fk"] = act(fk, bf, ACT.Exp, s1, scale=-1 / 16)
        y["fd"] = act(fd, fd, ACT.Exp, df, scale=1 / 16)
        bk = M[0]
        y["bk"] = act(bk, bq, ACT.Exp, dc, s1, scale=-1 / 16)
        y["bq"] = act(bq, bq, ACT.Exp, dc, y["bk"], scale=1 / 16)
        y["bd"] = act(bd_, bd_, ACT.Exp, dc, scale=1 / 16)
        ev = []
        for n in range(4):
            b = n % 2
            a = feat("gla_w_in", 256 * n, b, X)
            o = (q if n < 2 else k)
            o = o[:, 512 * (n % 2):512 * (n % 2) + 512]
            e = act(o, PS[:, b, :], ACT.Copy, a, scale=128 ** -0.5 if n < 2 else 1.0)
            pf[b] = [e]
            ev.append(e)

        def fill():
            for n in range(8):
                b = n % 2
                a = toks("gla_w_in", 1024 + 256 * n, b, X)
                o = v3(v if n < 4 else r, 2)[:, :, 256 * (n % 4):256 * (n % 4) + 256]
                e = act(o, v3(PS[:, b, :], 2), ACT.Copy if n < 4 else ACT.Silu, a)
                pf[b] = [e]
                if n == 3:
                    y["v"] = e
                if n >= 4:
                    g = sml("gog").unsqueeze(1).to_broadcast([128, 2, 256])
                    y["r"] = tt(PO, o, o, g, ALU.mult, e)
                yield

        fl = fill()
        z1 = tt(DV, fq, fq, q, ALU.mult, y["fq"], ev[1])
        z2 = tt(DV, fk, fk, k, ALU.mult, y["fk"], ev[3])
        z3 = tt(DV, fd, fd, k, ALU.mult, y["fd"])
        z4_ = tt(DV, bk, bk, k, ALU.mult, y["bk"])
        z5 = tt(DV, bq, bq, q, ALU.mult, y["bq"])
        z6 = tt(DV, bd_, bd_, k, ALU.mult, y["bd"])
        next(fl)
        ck = lambda ap, h, c: ap.rearrange("p (h c j) -> p h c j", h=4, c=4)[:, h, c, :]
        SCm = ar(0, 1024)
        SF, SB = ar(6144, 512), ar(10816, 512)
        kf2, qf2 = ar(1024, 512), ar(1536, 512)
        hv = lambda ap, c: ap.rearrange("p (h c j) -> p h c j", h=4, c=4)[:, :, c, :]
        h2 = lambda ap, c: ap.rearrange("p (h c j) -> p h c j", h=4, c=2)[:, :, c, :]
        tv = lambda ap, c: ap.rearrange("p (h c) -> p h c", h=4)[:, :, c:c + 1].to_broadcast([128, 4, 64])
        u = [tt(DV, h2(kf2, 0), hv(fd, 0), tv(totf, 1), ALU.mult, z6, x1),
             DV.do(lambda e: e.tensor_copy(h2(kf2, 1), hv(fd, 1))),
             DV.do(lambda e: e.tensor_copy(h2(qf2, 0), hv(fq, 2))),
             tt(DV, h2(qf2, 1), hv(fq, 3), tv(totf, 2), ALU.mult)]
        kb2, qb2 = ar(7232, 512), ar(7744, 512)
        u += [DV.do(lambda e: e.tensor_copy(h2(kb2, 0), hv(bd_, 2)), x2, y["fd"], y["bd"], y["fk"], y["fq"]),
              tt(DV, h2(kb2, 1), hv(bd_, 3), tv(totb, 2), ALU.mult),
              tt(DV, h2(qb2, 0), hv(bq, 0), tv(totb, 1), ALU.mult),
              DV.do(lambda e: e.tensor_copy(h2(qb2, 1), hv(bq, 1)))]
        for h in range(4):
            for blk in range(2):
                n = 2 * h + blk
                bank, col = 2 + n // 4, 128 * (n % 4)
                c0, c1 = 2 * blk, 2 * blk + 1
                PE.wait([z6, pf[2], pf[3]])
                lo, hi = slice(0, 64), slice(64, 128)
                mm(PS[lo, bank, col:col + 64], ck(fk, h, c0), ck(fq, h, c0), True, True)
                mm(PS[lo, bank, col + 64:col + 128], ck(fd, h, c0), ck(fq, h, c1), True, True)
                mm(PS[hi, bank, col:col + 64], ck(bd_, h, c1), ck(bq, h, c0), True, True)
                a = mm(PS[hi, bank, col + 64:col + 128], ck(fk, h, c1), ck(fq, h, c1), True, True, inc=(n in (3, 7)))
                if n == 3:
                    a0 = a
        a1 = a
        PE.wait(pf[4])
        for h in range(4):
            for blk in range(2):
                n = 2 * h + blk
                for c, rows in ((0, slice(0, 64)), (1, slice(64, 128))):
                    a = mm(PS[rows, 4, 64 * n:64 * n + 64], ck(bk, h, 2 * blk + c), ck(bq, h, 2 * blk + c),
                           True, True, inc=(n == 7 and c == 1))
        a2 = a
        next(fl)
        PE.wait([u[-1], pf[5], pf[6]])
        for h in range(4):
            mm(PS[:, 5, 128 * h:128 * h + 128], kf2[:, 128 * h:128 * h + 128], qf2[:, 128 * h:128 * h + 128], True, True)
            a = mm(PS[:, 6, 128 * h:128 * h + 128], kb2[:, 128 * h:128 * h + 128], qb2[:, 128 * h:128 * h + 128],
                   True, True, inc=(h == 3))
        a3 = a
        w1 = act(SCm[:, 0:512], PS[:, 2, :], ACT.Copy, a0, z5)
        w2 = act(SCm[:, 512:1024], PS[:, 3, :], ACT.Copy, a1)
        pf[2] = [w1]
        pf[3] = [w2]
        w3 = act(SF, PS[:, 5, :], ACT.Copy, a3, zt)
        w4 = act(SB, PS[:, 6, :], ACT.Copy, s2)
        pf[5] = [w3]
        pf[6] = [w4]
        mk = con("after64").bitcast(U32)
        for c, rows in ((0, slice(0, 64)), (1, slice(64, 128))):
            o = v3(SCm, 8)[rows, :, 64 * c:64 * c + 64]
            m_ = mk[rows, :].unsqueeze(1).to_broadcast([64, 8, 64])
            s_ = v3(PS[rows, 4, :], 8)
            w5 = DV.do(lambda e, o=o, m_=m_, s_=s_: e.copy_predicated(o, m_, s_), w1, w2, a2)
        pf[4] = [w5]
        for _ in range(2):
            next(fl)
        SC8, SF4, SB4 = v3(SCm, 8), v3(SF, 4), v3(SB, 4)
        V = v3(v, 2)
        ob = {}
        for tb in range(2):
            for h in range(4):
                bank = 2 + 2 * tb + h // 2
                if h % 2 == 0:
                    PE.wait([w5, w3, w4, y["v"], pf[bank]])
                o = PS[:, bank, 256 * (h % 2):256 * (h % 2) + 256]
                mm(o, SC8[:, 2 * h + tb, :], V[:, tb, 256 * h:256 * h + 256], True, False)
                side = SB4 if tb == 0 else SF4
                ob[(tb, h // 2)] = mm(o, side[:, h, :], V[:, 1 - tb, 256 * h:256 * h + 256], False, True, inc=(h % 2 == 1))
        drain(fl)
        return norm_gate(ob, 4, 256, lambda tb: v3(r, 2)[:, tb, :], y["r"])

    def norm_gate(ob, heads, w, gate, gdep, scale=None):
        n = 1024 // w
        ss = fresh(2 * n)
        for tb in range(2):
            for i in range(2):
                s = HS[:, tb, 512 * i:512 * i + 512]
                a = act(s, PS[:, 2 + 2 * tb + i, :], ACT.Square, ob[(tb, i)])
            a = DV.do(lambda e, tb=tb: e.tensor_reduce(ss[:, n * tb:n * tb + n], v3(HS[:, tb, :], n), AX, ALU.add), a)
        rr, a = rstd(ss, 2 * n, 1.0 / w, a)
        ot = []
        for tb in range(2):
            o = HS[:, tb, :]
            for i in range(2):
                b2 = rr[:, n * tb + n // 2 * i:n * tb + n // 2 * (i + 1)].unsqueeze(2).to_broadcast([128, n // 2, w])
                bank = 2 + 2 * tb + i
                b = tt(DV, v3(o[:, 512 * i:512 * i + 512], n // 2), v3(PS[:, bank, :], n // 2), b2, ALU.mult, a)
                pf[bank] = [b]
            if scale is None:
                ot.append(tt(DV, o, o, gate(tb), ALU.mult, b, gdep))
            else:
                ot.append(stt(v3(o, n), v3(o, n), scale, gate(tb), ALU.mult, ALU.mult, b))
        return turn(HS, 8, O, None, [6, 7, 2, 3], [], ot)

    def swiglu(layer):
        def up(i, of):
            a1 = feat(f"ffn_w_in{layer}", 256 * i, (2 * i) % 4, X, xt2)
            a2 = feat(f"ffn_w_in{layer}", 2816 + 256 * i, (2 * i + 1) % 4, X)
            b1, b2 = (2 * i) % 4, (2 * i + 1) % 4
            w = ar(512 * (i % 2), 512)
            a1 = act(w, PS[:, b1, :], ACT.Silu, a1)
            a = tt(DV, w, w, PS[:, b2, :], ALU.mult, a1, a2)
            pf[b1] = [a1]
            pf[b2] = [a]
            hi, lo = halves(i)
            c1_ = act(hi, w, ACT.Copy, a, of)
            return [c1_, tt(DV, lo, w, hi.bitcast(F32), ALU.subtract, c1_)]
        F = [PE.here(), DV.here(), AC.here()]
        AC.wait(F)
        DV.wait(F)
        return ffn(11, up, f"ffn_w_out{layer}", xt2, "")

    def ple(layer, ht):
        P = ar(1024, 512)
        F = [DV.here(), AC.here(), PE.here()]
        dp = SP.dma(lambda e: e.dma_start(P.rearrange("p (b d) -> p b d", b=2),
                                          io["p"][layer * 256:layer * 256 + 256, :].rearrange("(b p) d -> p b d", p=128)),
                    hw["d_p"], 16 * (layer + 1), F)
        pt = turn(v3(P, 2), 2, pair("O", 2, 0), None, [0, 1], PE.here(), dp)
        a = down(f"ple_w_proj{layer}", 0, pair("O", 2, 0), 0, [4, 5, 6, 7], True, True, pt)
        pw = ar(1536, 2048)
        for tb in range(2):
            for n in range(2):
                b = 4 + 2 * tb + n
                e = act(pw[:, 1024 * tb + 512 * n:1024 * tb + 512 * n + 512], PS[:, b, :], ACT.Copy, a, F)
                pf[b] = [e]
        xt = norm_turn(ht, sml(f"pn{layer}"), PE.here(), range(0, 4))
        g = ar(3584, 2048)
        t = []
        for n in range(4):
            b = n % 2
            a = toks(f"ple_w_gate{layer}", 256 * n, b, X, xt)
            gg = v3(g, 2)[:, :, 256 * n:256 * n + 256]
            a = act(gg, v3(PS[:, b, :], 2), ACT.Sigmoid, a, F)
            pf[b] = [a]
            a = tt(DV, gg, gg, v3(pw, 2)[:, :, 256 * n:256 * n + 256], ALU.mult, a, e)
            t.append(tt(DV, H[:, :, 256 * n:256 * n + 256], H[:, :, 256 * n:256 * n + 256], gg, ALU.add, a, xt))
        return t

    def diff(ht):
        xt = norm_turn(ht, sml("nm1"), PE.here())
        F = [PE.here(), DV.here(), AC.here(), PO.here()]
        for E in (AC, DV, PO):
            E.wait(F)
        w, ls = fresh(64), fresh(4)
        for i in range(2):
            a = tt(DV, w, sml(f"lq{i + 1}"), sml(f"lk{i + 1}"), ALU.mult, DV.here())
            a = DV.do(lambda e, i=i: e.tensor_reduce(ls[:, i:i + 1], w, AX, ALU.add), a)
        a = act(ls[:, 0:2], ls[:, 0:2], ACT.Exp, a)
        nlam = ls[:, 2:3]
        a = tt(DV, ls[:, 3:4], ls[:, 1:2], ls[:, 0:1], ALU.subtract, a)
        lt = ts(DV, nlam, ls[:, 3:4], -LAMBDA_INIT, None, ALU.add, None, a)
        tab = {}

        tt_ = []
        for qi, gname in enumerate(("gq", "gk")):
            g = sml(gname).rearrange("p (m a j) -> p m a j", m=2, a=2)
            for tb in range(2):
                pass
        tabs = ar(6144, 1024)
        n = 0
        for qi, gname in enumerate(("gq", "gk")):
            g = sml(gname).rearrange("p (m a j) -> p m a j", m=2, a=2)
            for tb in range(2):
                for x in range(4):
                    half = (0, 1, 1, 0)[x]
                    tbl = con("cos" if x in (0, 2) else "sin")[:, 32 * tb:32 * tb + 32].unsqueeze(1).to_broadcast([128, 2, 32])
                    o = tabs[:, 64 * n:64 * n + 64]
                    tt_.append(tt(PO, v3(o, 2), g[:, :, half, :], tbl, ALU.mult))
                    tab[(qi, tb, x)] = v3(o, 2)
                    n += 1
        qkT = [ar(0, 2048), ar(2048, 2048)]
        v = ar(4096, 2048)
        src = [ar(7168, 2048), ar(9216, 2048)]
        w1, w2 = ar(11264, 1024), ar(12288, 1024)
        n = 0
        ev = {}

        def gemm(sec, dst):
            nonlocal n
            e = []
            for i in range(4):
                b = n % 2
                n += 1
                a = toks("diff_w_in", sec * 1024 + 256 * i, b, X, xt)
                x = act(v3(dst, 2)[:, :, 256 * i:256 * i + 256], v3(PS[:, b, :], 2), ACT.Copy, a)
                pf[b] = [x]
                e.append(x)
                if sec == 2:
                    ev["v"] = x
                yield
            ev[sec] = x

        def shape(qi, fill):
            s = src[qi]
            S = v3(s, 2)
            ss = fresh(32)
            a = None
            for tb in range(2):
                a = act(w1, S[:, tb, :], ACT.Square, ev[qi], a)
                a = DV.do(lambda e, tb=tb: e.tensor_reduce(ss[:, 16 * tb:16 * tb + 16], v3(w1, 16), AX, ALU.add), a)
            r, a = rstd(ss, 32, 1.0 / 64, a)
            rd = None
            last = a
            for tb in range(2):
                b2 = r[:, 16 * tb:16 * tb + 16].unsqueeze(2).to_broadcast([128, 16, 64])
                a = tt(DV, v3(S[:, tb, :], 16), v3(S[:, tb, :], 16), b2, ALU.mult, last)
                x5 = S[:, tb, :].rearrange("p (h m a j) -> p h m a j", h=8, m=2, a=2)
                y5 = w1.rearrange("p (h m a j) -> p h m a j", h=8, m=2, a=2)
                z5 = w2.rearrange("p (h m a j) -> p h m a j", h=8, m=2, a=2)
                bt_ = lambda x: tab[(qi, tb, x)].unsqueeze(1).to_broadcast([128, 8, 2, 32])
                p = []
                for m in range(2):
                    tm = lambda x: tab[(qi, tb, x)][:, m, :].unsqueeze(1).to_broadcast([128, 8, 32])
                    p.append(tt(DV, y5[:, :, m, 0, :], x5[:, :, m, 0, :], tm(0), ALU.mult, a, tt_[-1], rd))
                    p.append(tt(PO, z5[:, :, m, 0, :], x5[:, :, m, 1, :], tm(1), ALU.mult, a, tt_[-1], rd))
                    p.append(tt(DV, y5[:, :, m, 1, :], x5[:, :, m, 1, :], tm(2), ALU.mult, a, rd))
                    p.append(tt(PO, z5[:, :, m, 1, :], x5[:, :, m, 0, :], tm(3), ALU.mult, a, tt_[-1], rd))
                xa = S[:, tb, :].rearrange("p (n a j) -> p n a j", n=16, a=2)
                ya = w1.rearrange("p (n a j) -> p n a j", n=16, a=2)
                za = w2.rearrange("p (n a j) -> p n a j", n=16, a=2)
                rd1 = tt(DV, xa[:, :, 0, :], ya[:, :, 0, :], za[:, :, 0, :], ALU.subtract, p)
                rd2 = tt(DV, xa[:, :, 1, :], ya[:, :, 1, :], za[:, :, 1, :], ALU.add, p)
                rd = [rd1, rd2]
                last = rd2
                next(fill, None)
            res = []
            for i in range(4):
                bank = 2 + i
                PE.wait([rd, pf[bank]])
                for j in range(2):
                    h = 2 * i + j
                    for tb in range(2):
                        a = tr(PS[:, bank, 256 * j + 128 * tb:256 * j + 128 * tb + 128], S[:, tb, 128 * h:128 * h + 128],
                               inc=(j == 1 and tb == 1))
                o = qkT[qi][:, 512 * i:512 * i + 512]
                if i % 2:
                    e = act(o, PS[:, bank, :], ACT.Copy, a)
                else:
                    e = DV.do(lambda e, o=o, bank=bank: e.tensor_copy(o, PS[:, bank, :]), a)
                pf[bank] = [e]
                res.append(e)
            return res

        drain(gemm(0, src[0]))
        gk = gemm(1, src[1])
        qr = shape(0, gk)
        drain(gk)
        gv = gemm(2, v)
        kr = shape(1, gv)
        drain(gv)
        Pm = [ar(7168 + 1024 * i, 1024) for i in range(3)]
        AT = [ar(10240 + 512 * i, 512) for i in range(3)]
        Aa = [ar(11776 + 512 * i, 512) for i in range(3)]
        mx, rs = fresh(32), fresh(32)
        cf = fresh(32)
        s1, s2, s3, s4, s5 = {}, {}, {}, {}, {}
        ob = {}
        QT, KT = v3(qkT[0], 8), v3(qkT[1], 8)
        V = v3(v, 2)

        def A(h):
            PE.wait([qr, kr])
            for m in range(2):
                bank = (0, 1) if h % 2 == 0 else (6, 7)
                bk = bank[m]
                rows = slice(64 * m, 64 * m + 64)
                for tb in range(2):
                    a = mm(PS[:, bk, 256 * tb:256 * tb + 256], QT[rows, h, 128 * tb:128 * tb + 128], KT[rows, h, :],
                           True, True, pf[bk], inc=(tb == 1))
                c = 4 * h + 2 * m
                x = DV.do(lambda e, c=c, bk=bk: e.tensor_reduce(mx[:, c:c + 2], v3(PS[:, bk, :], 2), AX, ALU.max), a)
                x = ts(DV, mx[:, c:c + 2], mx[:, c:c + 2], -0.125, None, ALU.mult, None, x)
                for tb in range(2):
                    o = Pm[h % 3][:, 512 * m + 256 * tb:512 * m + 256 * tb + 256]
                    y = act(o, PS[:, bk, 256 * tb:256 * tb + 256], ACT.Exp, x, s3.get(h - 3), bias=mx[:, c + tb:c + tb + 1],
                            scale=0.125, accum_out=rs[:, c + tb:c + tb + 1])
                pf[bk] = [x, y]
            s1[h] = y

        def B(h):
            c = 4 * h
            x = DV.do(lambda e: e.reciprocal(cf[:, c:c + 4], rs[:, c:c + 4]), s1[h])
            x = ts(DV, cf[:, c + 2:c + 4], cf[:, c + 2:c + 4], nlam, None, ALU.mult, None, x, lt)
            for tb in range(2):
                o = Aa[h % 3][:, 256 * tb:256 * tb + 256]
                p0 = Pm[h % 3][:, 256 * tb:256 * tb + 256]
                p1 = Pm[h % 3][:, 512 + 256 * tb:512 + 256 * tb + 256]
                y = ts(DV, o, p1, cf[:, c + 2 + tb:c + 3 + tb], None, ALU.mult, None, x, s4.get(h - 3))
                y = stt(o, p0, cf[:, c + tb:c + tb + 1], o, ALU.mult, ALU.add, y)
            s3[h] = y
            bank = (0, 1)[h % 2] if False else None
            return y

        def C(h):
            bank = TRB[h % 2]
            PE.wait([s3[h], pf[bank]])
            for sb_ in range(2):
                for tb in range(2):
                    a = tr(PS[:, bank, 256 * sb_ + 128 * tb:256 * sb_ + 128 * tb + 128],
                           Aa[h % 3][:, 256 * tb + 128 * sb_:256 * tb + 128 * sb_ + 128], inc=(sb_ == 1 and tb == 1))
            s4[h] = a
            o = AT[h % 3]
            if h % 2:
                e = act(o, PS[:, bank, :], ACT.Copy, a, s5.get(h - 3))
            else:
                e = DV.do(lambda e: e.tensor_copy(o, PS[:, bank, :]), a, s5.get(h - 3))
            pf[bank] = [e]
            s2[h] = e

        TRB = (1, 7)

        def Dd(h):
            at_ = v3(AT[h % 3], 2)
            PE.wait([s2[h]])
            for tb in range(2):
                bank = 2 + 2 * tb + h // 4
                if h % 4 == 0:
                    PE.wait(pf[bank])
                o = PS[:, bank, 128 * (h % 4):128 * (h % 4) + 128]
                mm(o, at_[:, 0, 128 * tb:128 * tb + 128], V[:, 0, 128 * h:128 * h + 128], True, False, ev["v"])
                a = mm(o, at_[:, 1, 128 * tb:128 * tb + 128], V[:, 1, 128 * h:128 * h + 128], False, True, inc=True)
                ob[(tb, h // 4)] = a
            s5[h] = a

        for i in range(11):
            if i < 8:
                A(i)
            if 1 <= i < 9:
                B(i - 1)
            if 2 <= i < 10:
                C(i - 2)
            if i >= 3:
                Dd(i - 3)
        gs = sml("gsub").unsqueeze(1).to_broadcast([128, 8, 128])
        return norm_gate(ob, 8, 128, lambda tb: gs, None, scale=1.0 - LAMBDA_INIT)

    if stage >= 2:
        ot = gla()
        ht = project("gla_w_out", O, ot, [0, 1, 2, 3])
    if stage >= 3:
        xt2 = norm_turn(ht, sml("nf0"), PE.here(), range(4, 8))
        ht = swiglu(0)
        ht = ple(0, ht)
    if stage >= 4:
        ot = diff(ht)
        ht = project("diff_w_out", O, ot, [0, 1, 2, 3])
        xt2 = norm_turn(ht, sml("nf1"), PE.here(), range(4, 8))
        ht = swiglu(1)
        ht = ple(1, ht)
    e = SP.dma(lambda e: e.dma_start(out.rearrange("(b p) d -> p b d", p=128), H), hw["d_out"], 16, ht)
    SP.wait([e])
    return {"SP": SP, "ACT": AC, "DVE": DV, "POOL": PO, "PE": PE}


STREAMED = {"w_in": "w_in", "w_o_sb": "w_o_sb", "w_o_hg": "w_o_hg", "w_out": "w_out", "w_ff1": "w_ff1",
            "w_ff2": "w_ff2", "gla_w_in": "gla_w_in_2", "gla_w_out": "gla_w_out_2",
            "diff_w_in": "diff_w_in_2", "diff_w_out": "diff_w_out_2"}
LAYERED = {"ffn_w_in": "ffn_w_in_2", "ffn_w_out": "ffn_w_out_2", "ple_w_gate": "ple_w_gate_2",
           "ple_w_proj": "ple_w_proj_2"}
STAGE = 4


def kernel(**inputs):
    import concourse.bacc as _bacc
    from concourse.bass_utils import run_bass_kernel_spmd as _run

    nc = _bacc.Bacc("TRN2", target_bir_lowering=False, num_devices=1)
    arrays, io = {}, {}

    def give(name, a):
        a = np.ascontiguousarray(a)
        arrays[f"in_{name}_dram"] = a
        io[name] = nc.dram_tensor(f"in_{name}_dram", a.shape, mybir.dt.from_np(a.dtype), kind="ExternalInput").ap()

    I = {k: np.asarray(v) for k, v in inputs.items()}
    for name, key in STREAMED.items():
        give(name, I[key][0])
    for name, key in LAYERED.items():
        for layer in range(2):
            give(f"{name}{layer}", I[key][layer])
    give("x", I["x"][0])
    give("p", I["p_2"].reshape(512, 256))
    give("const", constants()[0])
    col = lambda a: a.reshape(-1, 128).T
    row = lambda a: np.broadcast_to(a.reshape(1, -1), (128, a.size))
    small = {
        "g1": col(I["norm1_g"]), "g2": col(I["norm2_g"]), "bg": col(I["b_gate"]),
        "lb0": col(I["lb_logits"][0]), "lb1": col(I["lb_logits"][1]),
        "nm0": col(I["norm_mix_2"][0]), "nm1": col(I["norm_mix_2"][1]),
        "nf0": col(I["norm_ffn_2"][0]), "nf1": col(I["norm_ffn_2"][1]),
        "pn0": col(I["ple_norm_2"][0]), "pn1": col(I["ple_norm_2"][1]),
        "gbf": col(I["gla_b_gate_f_2"]), "gbb": col(I["gla_b_gate_b_2"]),
        "hgg": row(I["hg_norm_g"]), "gog": row(I["gla_g_out_2"]), "gq": row(I["diff_g_q_2"]),
        "gk": row(I["diff_g_k_2"]), "gsub": row(I["diff_g_sub_2"]), "lq1": row(I["diff_lam_q1_2"]),
        "lk1": row(I["diff_lam_k1_2"]), "lq2": row(I["diff_lam_q2_2"]), "lk2": row(I["diff_lam_k2_2"]),
    }
    give("small", np.concatenate([small[k] for k, _ in SMALL], axis=1))
    give("final", row(I["final_g"]))
    give("wgate", np.concatenate([I["gla_w_gate_f_2"][0], I["gla_w_gate_b_2"][0]], axis=1))
    out = nc.dram_tensor("out_0_dram", (256, 1024), F32, kind="ExternalOutput").ap()
    program(nc, io, out, STAGE)
    r = _run(nc, [arrays], core_ids=[0])
    return r.results[0]["out_0_dram"].reshape(1, 256, 1024)
```

```python
import math
from contextlib import ExitStack

import numpy as np
import concourse.bass as bass
from concourse import mybir

F32 = mybir.dt.float32
F32R = mybir.dt.float32r
BF16 = mybir.dt.bfloat16
U32 = mybir.dt.uint32
ALU = mybir.AluOpType
ACT = mybir.ActivationFunctionType
AX = mybir.AxisListType.X

T = 256
D = 1024
EPS = 1e-6
LAMBDA_INIT = 0.8 - 0.6 * math.exp(-0.3)

NR = 3
NW = 3
LOOK = 2
SLOT = 2048


def constants():
    p = np.arange(128)
    s, t = p[:, None], p[None, :]
    parts = {}
    parts["ident"] = (s == t)
    parts["ntri"] = -(s >= t).astype(np.float32)
    parts["none"] = -np.ones((128, 128))
    parts["before"] = (s < t)
    parts["neg"] = np.where(s < t, 0.0, -1e30)
    for n in range(7):
        m = 1 << n
        parts[f"lev{n}"] = (s // (2 * m) == t // (2 * m)) & (s % (2 * m) < m) & (t % (2 * m) >= m)
    parts["after64"] = (s % 64) > np.arange(64)[None, :]
    pos = np.arange(256, dtype=np.float32)
    inv = np.float32(10000.0) ** (-np.arange(32, dtype=np.float32) * np.float32(2.0) / np.float32(64))
    ang = (pos[:, None] * inv[None, :]).astype(np.float32)
    parts["cos"] = np.cos(ang).reshape(2, 128, 32).transpose(1, 0, 2).reshape(128, 64)
    parts["sin"] = np.sin(ang).reshape(2, 128, 32).transpose(1, 0, 2).reshape(128, 64)
    at, cols, off = {}, [], 0
    for k, v in parts.items():
        v = np.asarray(v, np.float32)
        at[k] = (off, off + v.shape[1])
        off += v.shape[1]
        cols.append(v)
    return np.ascontiguousarray(np.concatenate(cols, 1)), at


SMALL = [("g1", 8), ("g2", 8), ("bg", 16), ("lb0", 4), ("lb1", 4),
         ("nm0", 8), ("nm1", 8), ("nf0", 8), ("nf1", 8), ("pn0", 8), ("pn1", 8),
         ("gbf", 4), ("gbb", 4), ("hgg", 512), ("gog", 256), ("gq", 128), ("gk", 128),
         ("gsub", 128), ("lq1", 64), ("lk1", 64), ("lq2", 64), ("lk2", 64)]


def small_at():
    at, off = {}, 0
    for k, n in SMALL:
        at[k] = (off, off + n)
        off += n
    return at, off


class Engine:

    def __init__(self, sem):
        self.sem, self.n, self.ops, self.seen = sem, 0, [], {}

    def wait(self, after):
        for tok in after:
            if tok is None:
                continue
            if isinstance(tok, list):
                self.wait(tok)
                continue
            sem, val = tok
            if self.seen.get(id(sem), 0) < val:
                self.seen[id(sem)] = val
                self.ops.append(lambda e, sem=sem, val=val: e.wait_ge(sem, val))

    def do(self, fn, *after, inc=True):
        self.wait(after)
        if not inc:
            self.ops.append(fn)
            return None
        self.n += 1
        self.ops.append(lambda e: fn(e).then_inc(self.sem, 1))
        return (self.sem, self.n)

    def dma(self, fn, sem, val, *after):
        self.wait(after)
        self.ops.append(lambda e: fn(e).then_inc(sem, 16))
        return (sem, val)

    def here(self):
        return (self.sem, self.n)


class Turned:

    def __init__(self, step, nk):
        self.step, self.nk, self.n, self.toks = step, nk, 0, []

    def __len__(self):
        return self.nk

    def __getitem__(self, k):
        while self.n < min(k + 3, self.nk):
            self.toks.append(self.step(self.n))
            self.n += 1
        return self.toks[k]


class Joined(Turned):

    def __init__(self, a, b):
        self.a, self.b, self.nk = a, b, len(a) + len(b)

    @property
    def n(self):
        return self.a.n + self.b.n

    def __getitem__(self, k):
        return self.a[k] if k < len(self.a) else self.b[k - len(self.a)]


class Part(Turned):

    def __init__(self, whole, k0):
        self.whole, self.k0, self.nk = whole, k0, 2

    @property
    def n(self):
        return 0 if isinstance(self.whole, Turned) and self.whole.n < len(self.whole) else 2

    def __getitem__(self, k):
        return self.whole[self.k0 + k]


def program(nc, io, out, stage=4):
    plan = []
    with ExitStack() as ctx:
        hw = place(nc, ctx)
        emit(nc, hw, io, out, plan, None, stage)
        engines = emit(nc, hw, io, out, [], plan, stage)
        block = ctx.enter_context(nc.Block())

        @block.sync
        def _(e):
            for f in engines["SP"].ops:
                f(e)

        @block.scalar
        def _(e):
            for f in engines["ACT"].ops:
                f(e)

        @block.vector
        def _(e):
            for f in engines["DVE"].ops:
                f(e)

        @block.gpsimd
        def _(e):
            for f in engines["POOL"].ops:
                f(e)

        @block.tensor
        def _(e):
            for f in engines["PE"].ops:
                f(e)


def place(nc, ctx):
    def sb(name, shape, dt=F32):
        return ctx.enter_context(nc.sbuf_tensor(name, shape, dt))

    hw = {}
    nconst = constants()[0].shape[1]
    hw["CON"] = sb("CON", [128, nconst])
    hw["SML"] = sb("SML", [128, small_at()[1]])
    hw["IDB"] = sb("IDB", [128, 128], BF16)
    hw["NEGB"] = sb("NEGB", [128, 128], BF16)
    hw["SC"] = sb("SC", [128, 1000])
    hw["RAW"] = sb("RAW", [128, NR, SLOT])
    hw["WH"] = sb("WH", [128, NW, SLOT], F32R)
    hw["WL"] = sb("WL", [128, NW, SLOT], F32R)
    hw["XH"] = sb("XH", [128, 2048], F32R)
    hw["XL"] = sb("XL", [128, 2048], F32R)
    hw["OH"] = sb("OH", [128, 2048], F32R)
    hw["OL"] = sb("OL", [128, 2048], F32R)
    hw["H"] = sb("H", [128, 2048])
    hw["HS"] = sb("HS", [128, 2048])
    hw["AR"] = sb("AR", [128, 16960])
    hw["PTH"] = sb("PTH", [128, 512], F32R)
    hw["PTL"] = sb("PTL", [128, 512], F32R)
    hw["PS"] = ctx.enter_context(nc.psum_tensor("PS", [128, 8, 512], F32))
    for n in ("SP", "ACT", "DVE", "POOL", "PE"):
        hw["s" + n] = ctx.enter_context(nc.semaphore("s" + n))
    hw["raw"] = [ctx.enter_context(nc.semaphore(f"raw{i}")) for i in range(NR)]
    for n in ("con", "idn", "sml", "g1", "x0", "x1", "wg", "fg", "p", "out"):
        hw["d_" + n] = ctx.enter_context(nc.semaphore("d_" + n))
    return hw


def emit(nc, hw, io, out, said, plan, stage):
    SP, AC, DV, PO, PE = (Engine(hw["s" + n]) for n in ("SP", "ACT", "DVE", "POOL", "PE"))
    RAW, WH, WL, PS, AR, SC = hw["RAW"], hw["WH"], hw["WL"], hw["PS"], hw["AR"], hw["SC"]
    con_at = constants()[1]
    sml_at = small_at()[0]

    def con(k, rows=slice(0, 128)):
        a, b = con_at[k]
        return hw["CON"][rows, a:b]

    def sml(k):
        a, b = sml_at[k]
        return hw["SML"][:, a:b]

    def ar(off, n, rows=slice(0, 128)):
        assert off + n <= 16960
        return AR[rows, off:off + n]

    used = [0]

    def fresh(n):
        used[0] += n
        assert used[0] <= 1000
        return SC[:, used[0] - n:used[0]]

    pf = [[] for _ in range(8)]

    def act(o, i, f, *after, **kw):
        return AC.do(lambda e: e.activation(o, i, f, **kw), *after)

    def table(name):
        AC.ops.append(lambda e: e.preload_act_table_set(name))

    LOGEXP, SIGMOID, SILU = "natural_log_exp_and_others", "sigmoid_and_others", "silu_and_others"

    def tt(E, o, a, b, op, *after):
        return E.do(lambda e: e.tensor_tensor(o, a, b, op), *after)

    def ts(E, o, a, s1, s2, op0, op1, *after):
        if s2 is None:
            return E.do(lambda e: e.tensor_scalar(o, a, s1, None, op0), *after)
        return E.do(lambda e: e.tensor_scalar(o, a, s1, s2, op0, op1), *after)

    def stt(o, a, s, b, op0, op1, *after):
        return DV.do(lambda e: e.scalar_tensor_tensor(out=o, in0=a, scalar=s, in1=b, op0=op0, op1=op1), *after)

    def mm(o, l, r, start, stop, *after, inc=False, skip=False):
        return PE.do(lambda e: e.matmul(o, l, r, start=start, stop=stop, skip_group_check=skip),
                     *after, inc=inc)

    def mm3(o, s, m, start, stop, inc=False, skip=False):
        mm(o, s[0], m[0], start, False, skip=skip)
        mm(o, s[0], m[1], False, False, skip=skip)
        return mm(o, s[1], m[0], False, stop, inc=inc, skip=skip)

    def tr(o, i, *after, inc=False, k=128):
        return PE.do(lambda e: e.transpose(o, i, con("ident", slice(0, k))[:, 0:k]), *after, inc=inc)

    st = {"next": 0, "prep": 0, "h": [], "l": [], "pe": []}

    def prep(c):
        name, k0, nk, n0, nn = plan[c]
        src = io[name][k0 * 128:(k0 + nk) * 128, n0:n0 + nn].rearrange("(k p) n -> p k n", p=128)
        r, w, n = c % NR, c % NW, nk * nn
        dst = RAW[:, r, 0:n].rearrange("p (k n) -> p k n", k=nk)
        free = [st["h"][c - NR], st["l"][c - NR]] if c >= NR else []
        got = SP.dma(lambda e: e.dma_start(dst, src), hw["raw"][r], 16 * (c // NR + 1), free)
        idle = [st["pe"][c - NW]] if c >= NW else []
        wh, wl, raw = WH[:, w, 0:n], WL[:, w, 0:n], RAW[:, r, 0:n]
        h = act(wh, raw, ACT.Copy, got, idle)
        st["h"].append(h)
        st["l"].append(tt(DV, wl, raw, wh.bitcast(F32), ALU.subtract, got, h, idle))

    def preps(c):
        if plan is not None:
            while st["prep"] < min(c + LOOK + 1, len(plan)):
                prep(st["prep"])
                st["prep"] += 1

    def take(name, k0, nk, n0, nn, xt=()):
        c = st["next"]
        st["next"] += 1
        said.append((name, k0, nk, n0, nn))
        w = c % NW
        if plan is not None:
            if not (isinstance(xt, Turned) and xt.n < len(xt) and st["prep"] > c):
                preps(c)
            PE.wait([st["h"][c], st["l"][c]])
        view = [x[:, w, 0:nk * nn].rearrange("p (k n) -> p k n", k=nk) for x in (WH, WL)]
        return view

    def done(tok):
        st["pe"].append(tok)
        preps(len(st["pe"]) - 1)

    def pair(n, kt=8, base=0):
        return tuple(hw[n + s][:, base:base + kt * 256].rearrange("p (k t) -> p k t", k=kt) for s in "HL")

    X = pair("X")
    O = pair("O")

    def feat(name, n0, bank, ops, xt=(), *after):
        if len(xt):
            xt[0]
        w = take(name, 0, 8, n0, 256, xt)
        PE.wait([*after, pf[bank]])
        for k in range(8):
            if len(xt):
                PE.wait(xt[k])
            for fb in range(2):
                tok = mm3(PS[:, bank, fb * 256:fb * 256 + 256],
                          [x[:, k, fb * 128:fb * 128 + 128] for x in w], [x[:, k, :] for x in ops],
                          k == 0 and fb == 0, k == 7, inc=(fb == 1 and k == 7), skip=True)
        done(tok)
        return tok

    def toks(name, n0, bank, ops, xt=(), *after, nn=256):
        if len(xt):
            xt[0]
        w = take(name, 0, 8, n0, nn, xt)
        PE.wait([*after, pf[bank]])
        for k in range(8):
            if len(xt):
                PE.wait(xt[k])
            for tb in range(2):
                tok = mm3(PS[:, bank, tb * nn:tb * nn + nn],
                          [x[:, k, tb * 128:tb * 128 + 128] for x in ops], [x[:, k, :] for x in w],
                          k == 0 and tb == 0, k == 7, inc=(tb == 1 and k == 7), skip=True)
        done(tok)
        return tok

    def down(name, kt, ops, ok, banks, first, last, xt=()):
        if len(xt):
            xt[0]
        w = take(name, kt, 2, 0, 1024, xt)
        toks_ = []
        for tb in range(2):
            for k in range(2):
                if len(xt):
                    PE.wait(xt[k])
                for n in range(2):
                    if first and k == 0:
                        PE.wait(pf[banks[2 * tb + n]])
                    end = k == 1 and n == 1
                    tok = mm3(PS[:, banks[2 * tb + n], :],
                              [x[:, ok + k, tb * 128:tb * 128 + 128] for x in ops],
                              [x[:, k, n * 512:n * 512 + 512] for x in w],
                              first and k == 0, last and k == 1, inc=end)
            toks_.append(tok)
        done(tok)
        return toks_

    H = hw["H"][:, :].rearrange("p (b d) -> p b d", b=2)
    HS = hw["HS"][:, :].rearrange("p (b d) -> p b d", b=2)
    x_rows = io["x"].rearrange("(b p) d -> p b d", p=128)
    d_x = [SP.dma(lambda e, b=b: e.dma_start(H[:, b, :], x_rows[:, b, :]), hw[f"d_x{b}"], 16) for b in range(2)]
    nc0 = con_at["ident"][1]
    d_idn = AC.dma(lambda e: e.dma_start(hw["CON"][:, 0:nc0], io["const"][:, 0:nc0]), hw["d_idn"], 16)
    ns0 = 8
    d_g1 = AC.dma(lambda e: e.dma_start(hw["SML"][:, 0:ns0], io["small"][:, 0:ns0]), hw["d_g1"], 16)
    table(LOGEXP)

    def rstd(ss, n, inv, *after):
        ms, y, t = fresh(n), fresh(n), fresh(n)
        a = ts(DV, ms, ss, inv, EPS, ALU.mult, ALU.add, *after)
        a = act(y, ms, ACT.Ln, a)
        a = act(y, y, ACT.Exp, a, scale=-0.5)
        a = tt(DV, t, y, y, ALU.mult, a)
        a = stt(t, t, -0.5, ms, ALU.mult, ALU.mult, a)
        r = fresh(n)
        return r, stt(r, t, 1.5, y, ALU.add, ALU.mult, a)

    def rows_rstd(src, junk, dep):
        ss = fresh(4)
        for tb in range(2):
            for n in range(2):
                c = slice(512 * n, 512 * n + 512)
                a = act(junk[:, tb, c], src[:, tb, c], ACT.Square, dep[tb][n],
                        accum_out=ss[:, 2 * n + tb:2 * n + tb + 1])
        s2 = fresh(2)
        a = tt(DV, s2, ss[:, 0:2], ss[:, 2:4], ALU.add, a)
        return rstd(s2, 2, 1.0 / D, a)

    def split_evac(bank, n, hi, lo, g, *after):
        src = PS[:, bank, 0:n]
        a = act(hi, src, ACT.Copy, *after, **({} if g is None else {"scale": g}))
        if g is None:
            b = tt(DV, lo, src, hi.bitcast(F32), ALU.subtract, a)
        else:
            b = stt(lo, src, g, hi.bitcast(F32), ALU.mult, ALU.subtract, a)
        pf[bank] = [a, b]
        return [a, b]

    def turn(src, nk, dst, gains, banks, free, dep):
        def step(k):
            bank = banks[k % len(banks)]
            PE.wait([dep(k), pf[bank]])
            tr(PS[:, bank, 0:128], src[:, 0, k * 128:k * 128 + 128])
            a = tr(PS[:, bank, 128:256], src[:, 1, k * 128:k * 128 + 128], inc=True)
            g = None if gains is None else gains[:, k:k + 1]
            return split_evac(bank, 256, dst[0][:, k, :], dst[1][:, k, :], g, a, free)
        return Turned(step, nk)

    def norm_turn(dep, gains, xfree, banks=range(4, 8)):
        r, a = rows_rstd(H, HS, dep)
        t = []
        for n in range(2):
            c = slice(512 * n, 512 * n + 512)
            t.append([ts(DV, HS[:, tb, c], H[:, tb, c], r[:, tb:tb + 1], None, ALU.mult, None, a) for tb in range(2)])
        return turn(HS, 8, X, gains, list(banks), xfree, lambda k: t[k // 4])

    v3 = lambda ap, a: ap.rearrange("p (a b) -> p a b", a=a)

    PE.wait([d_idn])
    xt = norm_turn([[d_x[0]] * 2, [d_x[1]] * 2], sml("g1"), [])
    AC.wait([d_g1])
    DV.wait([d_g1])
    wgate = ar(15936, 1024, slice(0, 16))
    d_con = AC.dma(lambda e: e.dma_start(hw["CON"][:, nc0:], io["const"][:, nc0:]), hw["d_con"], 16)
    d_sml = AC.dma(lambda e: e.dma_start(hw["SML"][:, ns0:], io["small"][:, ns0:]), hw["d_sml"], 16)
    d_wg = AC.dma(lambda e: e.dma_start(wgate, io["wgate"]), hw["d_wg"], 16)
    if plan is not None:
        prep(0)
        st["prep"] = 1

    def mixers():
        qT, kT, v = (ar(o, 1024) for o in (0, 1024, 2048))
        kh, qh, lf, bb, vh, GS, fr, ng = (ar(6528 + 1024 * i, 1024) for i in range(8))
        got = {}

        def evac(o, b, a, *after, **kw):
            e = act(o, v3(PS[:, b, :], 2), ACT.Copy, a, *after, **kw)
            pf[b] = [e]
            return e

        def chunks():
            n = 0
            rows = lambda d, i: v3(d, 4)[:, 2 * i:2 * i + 2, :]
            cols = lambda d, i: v3(d, 2)[:, :, 256 * i:256 * i + 256]
            for sec, key, dst, f, view in ((0, "q", qT, feat, rows), (512, "k", kT, feat, rows),
                                           (1024, "v", v, toks, cols), (1536, "f", fr, feat, rows),
                                           (2560, "qh", qh, feat, rows), (3072, "g", GS, toks, cols),
                                           (2048, "vh", vh, toks, cols)):
                for i in range(2):
                    b = n % 2
                    n += 1
                    a = f("w_in", sec + 256 * i, b, X, xt)
                    got[key] = evac(view(dst, i), b, a, scale=0.125 if sec == 0 else 1.0)
                    yield
            for i in range(8):
                b = n % 2
                n += 1
                a = feat("w_in", 3584 + 256 * i, b, X)
                dst = ar(2048 * (i // 4), 2048)
                for j in range(2):
                    e = act(v3(dst, 8)[:, 2 * (i % 4) + j, :], PS[:, b, 256 * j:256 * j + 256], ACT.Identity, a,
                            got["oT"] if i >= 4 else got["s"], bias=sml("bg")[:, 2 * i + j:2 * i + j + 1])
                pf[b] = [e]
                got["gates"] = e
                yield

        fill = chunks()
        go = lambda n=1: [next(fill, None) for _ in range(n)]

        V = v3(v, 2)
        work = lambda i, j: ar(3072 + 1152 * (i % 3) + 384 * j, 384)
        t0, t1, t2, wf = {}, {}, {}, {}
        osb = []

        def sA(h):
            j, base, z = h // 2, 64 * (h % 2), 2 + h % 2
            q = v3(qT, 4)[base:base + 64, j, :]
            k = v3(kT, 4)[base:base + 64, j, :]
            mm(PS[:, z, 0:256], k[:, 0:128], q, True, True, got["q"], got["k"], pf[z])
            a = mm(PS[:, z, 256:384], k[:, 128:256], q[:, 128:256], False, True, inc=True, skip=True)
            got["s"] = a
            e, sp = work(h, 0), work(h, 1)
            Z = PS[:, z, 0:384]
            a1 = act(e, Z, ACT.Abs, a, wf.get(h - 3))
            a1 = act(e, e, ACT.Exp, a1, scale=-1.0)
            a1 = act(e, e, ACT.Ln, a1, bias=1.0)
            a2 = stt(sp, Z, 0.0, e, ALU.max, ALU.add, a1, t1.get(h - 3))
            dg = sp[:, 0:384].rearrange("p (a b) -> p a b", a=3)[:, 0:3:2, :]
            mk = con("before").unsqueeze(1).to_broadcast([128, 2, 128])
            t0[h] = tt(DV, dg, dg, mk, ALU.mult, a2)

        def sB(h):
            z = 2 + h % 2
            sp, w = work(h, 1), work(h, 2)
            mm(PS[:, z, 0:384], con("ntri"), sp, False, True, t0[h], skip=True)
            mm(PS[:, z, 128:256], con("none"), sp[:, 256:384], False, True, skip=True)
            mm(PS[:, z, 0:128], hw["IDB"][:, :], hw["NEGB"][:, :], False, True, skip=True)
            t1[h] = mm(PS[:, z, 256:384], hw["IDB"][:, :], hw["NEGB"][:, :], False, True, inc=True, skip=True)
            t2[h] = act(w, PS[:, z, 0:384], ACT.Exp, t1[h], wf.get(h - 3))
            pf[z] = [t2[h]]

        def sC(h):
            j, base, ob = h // 2, 64 * (h % 2), 4
            w = work(h, 2)
            o = PS[base:base + 64, ob, 0:256]
            if h % 2 == 0:
                PE.wait(pf[ob])
            mm(o, V[:, 0, h * 64:h * 64 + 64], w[:, 0:256], True, True, t2[h], got["v"])
            wf[h] = mm(PS[base:base + 64, ob, 128:256], V[:, 1, h * 64:h * 64 + 64], w[:, 256:384],
                       False, True, inc=True, skip=True)
            if h == 7:
                got["oT"] = wf[h]
            if h % 2 == 1:
                hi, lo = (hw["O" + x][:, j * 256:j * 256 + 256] for x in "HL")
                osb.append(split_evac(ob, 256, hi, lo, None, wf[h]))

        def stick(i):
            if 1 <= i < 9:
                sB(i - 1)
            if 0 <= i < 8:
                sA(i)
            if 2 <= i < 10:
                sC(i - 2)

        go(2)
        AC.wait([d_sml])
        DV.wait([d_con, d_sml])
        c1 = DV.do(lambda e: e.tensor_copy(hw["IDB"][:, :], con("ident")))
        c2 = DV.do(lambda e: e.tensor_copy(hw["NEGB"][:, :], con("neg")))
        PE.wait([c1, c2])

        lb, oml, w8 = fresh(4), fresh(4), fresh(12)
        a = tt(DV, w8[:, 0:4], sml("lb0"), sml("lb1"), ALU.max)
        a1 = tt(DV, w8[:, 4:8], sml("lb0"), w8[:, 0:4], ALU.subtract, a)
        a2 = tt(DV, w8[:, 8:12], sml("lb1"), w8[:, 0:4], ALU.subtract, a)
        lbx = act(w8[:, 4:12], w8[:, 4:12], ACT.Exp, a1, a2)
        a = tt(DV, w8[:, 0:4], w8[:, 4:8], w8[:, 8:12], ALU.add, lbx)
        a = DV.do(lambda e: e.reciprocal(w8[:, 0:4], w8[:, 0:4]), a)
        a = tt(DV, lb, w8[:, 4:8], w8[:, 0:4], ALU.mult, a)
        lbt = ts(DV, oml, lb, -1.0, 1.0, ALU.mult, ALU.add, a)

        E_ = [HS[:, 0, :], HS[:, 1, :]]
        P_ = [fr, ng]
        ACC = ar(14720, 1024)
        ACC2 = lf[:, 0:512]
        A8 = v3(ACC, 8)
        HB = (5, 6)
        et, ptk, ex = {}, {}, {}
        st2 = {}

        def h_gate():
            table(SIGMOID)
            a2 = act(ng, fr, ACT.Sigmoid, got["f"], scale=-1.0)
            a1 = act(fr, fr, ACT.Sigmoid, a2)
            sq, sg = HS[:, 0, :], HS[:, 1, :]
            b1 = act(sq, qh, ACT.Sigmoid, got["qh"])
            b2 = act(sg, GS, ACT.Sigmoid, got["g"])
            table(LOGEXP)
            for h in range(4):
                f1 = ts(DV, v3(lf, 4)[:, h, :], v3(fr, 4)[:, h, :], oml[:, h:h + 1], lb[:, h:h + 1],
                        ALU.mult, ALU.add, a1, lbt)
                f2 = ts(DV, v3(kh, 4)[:, h, :], v3(ng, 4)[:, h, :], oml[:, h:h + 1], None, ALU.mult, None, a2)
            one128 = ACC
            m1 = PO.do(lambda e: e.memset(one128, 1.0))
            m1 = PO.do(lambda e: e.memset(v3(one128, 8)[:, :, 0:1], 0.0), m1)
            a = act(lf, lf, ACT.Ln, f1)
            st2["qh"] = tt(DV, qh, qh, sq, ALU.mult, b1)
            st2["g"] = tt(PO, GS, GS, sg, ALU.mult, b2)
            gb = sml("hgg").unsqueeze(1).to_broadcast([128, 2, 512])
            st2["g"] = tt(PO, v3(GS, 2), v3(GS, 2), gb, ALU.mult, st2["g"])
            st2["b"] = DV.do(lambda e: e.tensor_tensor_scan(bb, one128, lf, 0.0, ALU.mult, ALU.add), a, m1)
            st2["k"] = f2

        def h_diag():
            for j in range(8):
                a = mm(PS[:, HB[j // 4], 128 * (j % 4):128 * (j % 4) + 128], v3(kh, 8)[:, j, :],
                       v3(qh, 8)[:, j, :], True, True, st2["qh"], st2["k"], pf[HB[0]], pf[HB[1]], inc=(j == 7))
            idb = con("ident").unsqueeze(1).to_broadcast([128, 8, 128])
            src = PS[:, HB[0]:HB[0] + 2, :].rearrange("p a (b c) -> p (a b) c", c=128)
            acc = tt(DV, A8, src, idb, ALU.mult, a, st2["b"])
            pf[HB[0]] = [acc]
            pf[HB[1]] = [acc]
            st2["acc"] = acc

        def cutm(ap, m):
            return ap.rearrange("p (n m) -> p n m", m=2 * m)

        def h1(lv):
            E = E_[lv % 2]
            prev = [ptk.get(lv - 2), st2["g"], st2["qh"]]
            if lv < 7:
                m = 1 << lv
                B = cutm(bb, m)
                first, second = slice(0, m), slice(m, 2 * m)
                ref = B[:, :, m - 1:m].to_broadcast([128, 1024 // (2 * m), m])
                a1 = tt(DV, cutm(E, m)[:, :, second], B[:, :, second], ref, ALU.subtract, st2["b"], prev)
                a2 = tt(DV, cutm(E, m)[:, :, first], ref, B[:, :, first], ALU.subtract, prev)
            else:
                B = v3(bb, 4)
                a1 = tt(DV, v3(E, 4)[:, :, 0:128], B[:, :, 127:128].to_broadcast([128, 4, 128]), B[:, :, 0:128],
                        ALU.subtract, prev)
                a2 = DV.do(lambda e: e.tensor_copy(v3(E, 4)[:, :, 128:256], B[:, :, 128:256]), prev)
            ex[lv] = act(E, E, ACT.Exp, a1, a2)

        def h2(lv):
            E, P = E_[lv % 2], P_[lv % 2]
            m = 1 << lv
            first, second = slice(0, m), slice(m, 2 * m)
            w = [ex[lv], et.get(lv - 2), st2["b"]]
            e1 = tt(PO, cutm(P, m)[:, :, second], cutm(E, m)[:, :, second], cutm(qh, m)[:, :, second], ALU.mult, w)
            e2 = tt(DV, cutm(P, m)[:, :, first], cutm(E, m)[:, :, first], cutm(kh, m)[:, :, first], ALU.mult, w)
            ptk[lv] = [e1, e2]

        def h3(lv):
            P = P_[lv % 2]
            if lv < 7:
                for j in range(8):
                    a = mm(PS[:, HB[j // 4], 128 * (j % 4):128 * (j % 4) + 128], v3(P, 8)[:, j, :],
                           v3(P, 8)[:, j, :], True, True, ptk[lv], pf[HB[0]], pf[HB[1]], inc=(j == 7))
            else:
                for h in range(4):
                    a = mm(PS[:, 7, 128 * h:128 * h + 128], v3(P, 4)[:, h, 0:128], v3(P, 4)[:, h, 128:256],
                           True, True, ptk[lv], pf[7], inc=(h == 3))
            et[lv] = a

        def h4(lv):
            if lv < 7:
                src = PS[:, HB[0]:HB[0] + 2, :].rearrange("p a (b c) -> p (a b) c", c=128)
                mk = con(f"lev{lv}").bitcast(U32).unsqueeze(1).to_broadcast([128, 8, 128])
                acc = DV.do(lambda e: e.copy_predicated(A8, mk, src), et[lv], st2["acc"])
                pf[HB[0]] = [acc]
                pf[HB[1]] = [acc]
                st2["acc"] = acc
            else:
                st2["acc2"] = act(ACC2, PS[:, 7, :], ACT.Copy, et[lv], st2["b"])
                pf[7] = [st2["acc2"]]

        def hgrn(n):
            if 0 <= n - 3 < 8:
                h4(n - 3)
            if 0 <= n < 8:
                h1(n)
            if 0 <= n - 2 < 8:
                h3(n - 2)
            if 0 <= n - 1 < 8:
                h2(n - 1)

        go(4)
        for i in range(10):
            stick(i)
            if i == 6:
                h_gate()
            if i == 7:
                h_diag()
            if i >= 8:
                hgrn(i - 8)
            go()
        for n in range(2, 11):
            hgrn(n)
            if n < 8:
                go()
        VH = v3(vh, 2)
        OB = (6, 7)
        o_t = []
        for tb in range(2):
            PE.wait([st2["acc"], st2["acc2"], got["vh"], pf[OB[tb]]])
            for h in range(4):
                o = PS[:, OB[tb], 128 * h:128 * h + 128]
                a = mm(o, A8[:, 2 * h + tb, :], VH[:, tb, 128 * h:128 * h + 128], True, tb == 0, inc=(h == 3 and tb == 0))
                if tb == 1:
                    a = mm(o, v3(ACC2, 4)[:, h, :], VH[:, 0, 128 * h:128 * h + 128], False, True, inc=(h == 3))
            o_t.append(a)
        og = norm_half(OB, 0, 4, o_t, lambda tb, h: v3(GS, 2)[:, tb, 128 * h:128 * h + 128], st2["g"])
        table(SIGMOID)
        gs = []
        for i in range(4):
            g = ar(1024 * i, 1024)
            gs.append(act(g, g, ACT.Sigmoid, got["gates"]))
        table(LOGEXP)
        return osb, og, gs, fill

    def norm_half(banks, half, heads, o_t, gate, gdep, scale=None):
        w = 512 // heads
        c = slice(512 * half, 512 * half + 512)
        ss = fresh(2 * heads)
        for tb in range(2):
            a = act(HS[:, tb, c], PS[:, banks[tb], :], ACT.Square, o_t[tb], hs_free[0])
            a = DV.do(lambda e, tb=tb: e.tensor_reduce(ss[:, heads * tb:heads * tb + heads],
                                                       v3(HS[:, tb, c], heads), AX, ALU.add), a)
        rr, a = rstd(ss, 2 * heads, 1.0 / w, a)
        if scale is not None:
            a = ts(DV, rr, rr, scale, None, ALU.mult, None, a)
        out_ = []
        for tb in range(2):
            for h in range(heads):
                n = heads * tb + h
                b = stt(HS[:, tb, 512 * half + w * h:512 * half + w * h + w], PS[:, banks[tb], w * h:w * h + w],
                        rr[:, n:n + 1], gate(tb, heads * half + h), ALU.mult, ALU.mult, a, gdep)
            pf[banks[tb]] = [b]
        return b

    hs_free = [None]
    osb_t, og, gs, fill = mixers()

    OS, OG = pair("O", 4, 0), pair("O", 4, 1024)
    ga, gb_, mg = ar(0, 2048), ar(2048, 2048), ar(4096, 2048)

    def out_feat(name, ops, c, b0, dep):
        w = take(name, 0, 4, 512 * c, 512)
        PE.wait([pf[b0], pf[b0 + 1]])
        for k in range(4):
            PE.wait(dep[k])
            for fb in range(4):
                a = mm3(PS[:, b0 + fb // 2, 256 * (fb % 2):256 * (fb % 2) + 256],
                        [x[:, k, fb * 128:fb * 128 + 128] for x in w], [x[:, k, :] for x in ops],
                        k == 0 and fb % 2 == 0, k == 3, inc=(fb == 3 and k == 3), skip=True)
        done(a)
        return a

    for _ in fill:
        pass
    sa = [out_feat("w_o_sb", OS, 0, 0, osb_t), out_feat("w_o_sb", OS, 1, 4, osb_t)]
    ohg_t = turn(HS[:, :, 0:512], 4, OG, None, [6, 7], [], lambda k: og)
    sg_ = [out_feat("w_o_hg", OG, 0, 2, ohg_t), out_feat("w_o_hg", OG, 1, 6, ohg_t)]
    mt = []
    for c in range(2):
        for i in range(2):
            g1 = ga[:, 1024 * c + 512 * i:1024 * c + 512 * i + 512]
            g2 = gb_[:, 1024 * c + 512 * i:1024 * c + 512 * i + 512]
            o = mg[:, 1024 * c + 512 * i:1024 * c + 512 * i + 512]
            ba, bg2 = 4 * c + i, (2, 6)[c] + i
            a1 = tt(DV, g1, g1, PS[:, ba, :], ALU.mult, sa[c], gs[c])
            a2 = tt(DV, g2, g2, PS[:, bg2, :], ALU.mult, sg_[c], gs[2 + c])
            pf[ba] = [a1]
            pf[bg2] = [a2]
            a = tt(DV, o, g1, g2, ALU.add, a1, a2)
            hi, lo = (hw["X" + s][:, 1024 * c + 512 * i:1024 * c + 512 * i + 512] for s in "HL")
            b = act(hi, o, ACT.Copy, a, sg_[0])
            b = [b, tt(DV, lo, o, hi.bitcast(F32), ALU.subtract, b)]
            mt += [b, b]
    fg = ar(6528, 1024)
    d_fg = SP.dma(lambda e: e.dma_start(fg, io["final"]), hw["d_fg"], 16, ohg_t[3])

    def residual(banks, a):
        t = []
        for tb in range(2):
            t.append([])
            for n in range(2):
                b = banks[2 * tb + n]
                o = H[:, tb, 512 * n:512 * n + 512]
                e = tt(DV, o, o, PS[:, b, :], ALU.add, a[tb])
                pf[b] = [e]
                t[tb].append(e)
        return t

    def project(name, ops, dep, banks):
        for i in range(4):
            a = down(name, 2 * i, ops, 2 * i, banks, i == 0, i == 3, Part(dep, 2 * i))
        return residual(banks, a)

    ht = project("w_out", X, mt, [0, 1, 2, 3])

    def ffn(n, up, dname):
        ready, of = {}, {}
        for i in range(n + 1):
            if i < n:
                ready[i] = up(i, of.get(i - 2))
            if i >= 1:
                j = i - 1
                s = j % 2
                ops = tuple(v3(x, 8)[:, 2 * s:2 * s + 2, :] for x in (hw["OH"][:, :], hw["OL"][:, :]))
                of[j] = down(dname, 2 * j, ops, 0, [4, 5, 6, 7], j == 0, j == n - 1, [ready[j], []])
        return of[n - 1]

    def halves(i):
        s = i % 2
        return tuple(hw["O" + x][:, 512 * s:512 * s + 512] for x in "HL")

    xt = norm_turn(ht, sml("g2"), PE.here(), range(4, 8))

    def up_relu(i, of):
        b = i % 4
        a = feat("w_ff1", 256 * i, b, X, xt)
        w = ar(512 * (i % 2), 512)
        a = ts(DV, w, PS[:, b, :], 0.0, None, ALU.max, None, a)
        pf[b] = [a]
        a = act(w, w, ACT.Square, a)
        hi, lo = halves(i)
        b1 = act(hi, w, ACT.Copy, a, of)
        b2 = tt(DV, lo, w, hi.bitcast(F32), ALU.subtract, b1)
        return [b1, b2]

    ht = residual([4, 5, 6, 7], ffn(16, up_relu, "w_ff2"))
    r, a = rows_rstd(H, HS, ht)
    ht = []
    for tb in range(2):
        ht.append([])
        for n in range(2):
            c = slice(512 * n, 512 * n + 512)
            ht[tb].append(stt(H[:, tb, c], H[:, tb, c], r[:, tb:tb + 1], fg[:, c], ALU.mult, ALU.mult, a, d_fg))

    def gla():
        xt = norm_turn(ht, sml("nm0"), PE.here())
        q, k = ar(0, 1024), ar(1024, 1024)
        v, r = ar(2048, 2048), ar(4096, 2048)
        a = toks("gla_w_in", 3072, 2, X, xt, nn=32)
        z = ar(6144, 64)
        a = act(z, PS[:, 2, 0:64], ACT.Copy, a)
        pf[2] = [a]
        z4 = z.rearrange("p (t d r) -> p t d r", t=2, d=2)
        zT = ar(6208, 512, slice(0, 16))
        y = {}

        def chunks():
            for n in range(12):
                b = n % 2
                if n < 4:
                    a = feat("gla_w_in", 256 * n, b, X)
                    o = (q if n < 2 else k)[:, 512 * (n % 2):512 * (n % 2) + 512]
                    y[("q", "k")[n // 2]] = act(o, PS[:, b, :], ACT.Copy, a, scale=128 ** -0.5 if n < 2 else 1.0)
                    pf[b] = [y[("q", "k")[n // 2]]]
                    yield
                    continue
                a = toks("gla_w_in", 256 * n, b, X)
                o = v3(v if n < 8 else r, 2)[:, :, 256 * (n % 4):256 * (n % 4) + 256]
                if n == 8:
                    table(SILU)
                e = act(o, v3(PS[:, b, :], 2), ACT.Copy if n < 8 else ACT.Silu, a)
                if n == 11:
                    table(LOGEXP)
                pf[b] = [e]
                if n < 8:
                    y["v"] = e
                else:
                    g = sml("gog").unsqueeze(1).to_broadcast([128, 2, 256])
                    y["r"] = tt(PO if n < 11 else DV, o, o, g, ALU.mult, e)
                    if n == 10:
                        y["r2"] = y["r"]
                yield

        fill = chunks()
        go = lambda n=1: [next(fill, None) for _ in range(n)]
        go(1)
        PE.wait([a, pf[3]])
        for d in range(2):
            for tb in range(2):
                a = tr(PS[0:16, 3, 256 * d + 128 * tb:256 * d + 128 * tb + 128], z4[:, tb, d, :], inc=(d == 1 and tb == 1))
        zt = act(zT, PS[0:16, 3, :], ACT.Copy, a)
        pf[3] = [zt]
        wg = wgate.rearrange("p (d n) -> p d n", d=2)
        L = [ar(6720, 1024), ar(7744, 1024)]
        M = [ar(8768, 1024), ar(9792, 1024)]
        ls = []
        for d in range(2):
            bs = [4, 5] if d == 0 else [6, 7]
            PE.wait([zt, d_wg, pf[bs[0]], pf[bs[1]]])
            for h in range(4):
                a = mm(PS[:, bs[h // 2], 256 * (h % 2):256 * (h % 2) + 256], wg[:, d, 128 * h:128 * h + 128],
                       zT[:, 256 * d:256 * d + 256], True, True, inc=(h == 3))
            for h in range(4):
                src = PS[:, bs[h // 2], 256 * (h % 2):256 * (h % 2) + 256]
                bias = sml("gbf" if d == 0 else "gbb")[:, h:h + 1]
                e2 = ts(DV, M[d][:, 256 * h:256 * h + 256], src, bias, None, ALU.add, None, a)
            pf[bs[0]] = [e2]
            pf[bs[1]] = [e2]
            e1 = act(L[d], M[d], ACT.Abs, e2)
            e1 = act(L[d], L[d], ACT.Exp, e1, scale=-1.0)
            e1 = act(L[d], L[d], ACT.Ln, e1, bias=1.0)
            ls.append(stt(M[d], M[d], 0.0, L[d], ALU.min, ALU.subtract, e1))
            go(1)
        one64 = ar(10816, 1024)
        a1 = PO.do(lambda e: e.memset(one64, 1.0), zt)
        a1 = PO.do(lambda e: e.memset(v3(one64, 16)[:, :, 0:1], 0.0), a1)
        bf, bp = L
        s1 = DV.do(lambda e: e.tensor_tensor_scan(bf, one64, M[0], 0.0, ALU.mult, ALU.add), ls[0], a1)
        s2 = DV.do(lambda e: e.tensor_tensor_scan(bp, one64, M[1], 0.0, ALU.mult, ALU.add), ls[1])
        c16 = lambda ap: v3(ap, 16)
        tot = lambda ap: c16(ap)[:, :, 63:64].to_broadcast([128, 16, 64])
        totf, totb = fresh(16), fresh(16)
        ends = lambda ap: c16(ap)[:, :, 63:64].rearrange("p c j -> p (c j)")
        fq, fk, fd = ar(11840, 1024), ar(12864, 1024), ar(13888, 1024)
        df = tt(DV, c16(fd), tot(bf), c16(bf), ALU.subtract, s1)
        bd_ = M[1]
        db = tt(DV, bd_, bp, M[1], ALU.subtract, s2)
        bq = ar(14912, 1024)
        dc = tt(DV, c16(bq), tot(bp), c16(bd_), ALU.subtract, db)
        go(1)
        y["fq"] = act(fq, bf, ACT.Exp, s1, scale=1 / 16)
        y["fk"] = act(fk, bf, ACT.Exp, s1, scale=-1 / 16)
        y["fd"] = act(fd, fd, ACT.Exp, df, scale=1 / 16)
        go(1)
        x1 = act(totf, ends(bf), ACT.Exp, s1, scale=1 / 16)
        x2 = act(totb, ends(bp), ACT.Exp, s2, scale=1 / 16)
        bk = M[0]
        y["bk"] = act(bk, bq, ACT.Exp, dc, s1, scale=-1 / 16)
        y["bq"] = act(bq, bq, ACT.Exp, dc, y["bk"], scale=1 / 16)
        y["bd"] = act(bd_, bd_, ACT.Exp, dc, scale=1 / 16)
        z1 = tt(DV, fq, fq, q, ALU.mult, y["fq"], y["q"])
        z2 = tt(PO, fk, fk, k, ALU.mult, y["fk"], y["k"])
        z3 = tt(DV, fd, fd, k, ALU.mult, y["fd"], y["k"])
        go(1)
        z4_ = tt(DV, bk, bk, k, ALU.mult, y["bk"])
        z5 = tt(PO, bq, bq, q, ALU.mult, y["bq"], y["q"])
        z6 = tt(DV, bd_, bd_, k, ALU.mult, y["bd"])
        go(1)
        ck = lambda ap, h, c: ap.rearrange("p (h c j) -> p h c j", h=4, c=4)[:, h, c, :]
        SCm = ar(0, 1024)
        SF, SB = ar(6144, 512), ar(10816, 512)
        kf2, qf2 = ar(1024, 512), ar(1536, 512)
        kb2, qb2 = ar(7232, 512), ar(7744, 512)
        hv = lambda ap, c: ap.rearrange("p (h c j) -> p h c j", h=4, c=4)[:, :, c, :]
        h2 = lambda ap, c: ap.rearrange("p (h c j) -> p h c j", h=4, c=2)[:, :, c, :]
        tv = lambda ap, c: ap.rearrange("p (h c) -> p h c", h=4)[:, :, c:c + 1].to_broadcast([128, 4, 64])
        for h in range(4):
            for blk in range(2):
                n = 2 * h + blk
                bank, col = 2 + n // 4, 128 * (n % 4)
                c0, c1 = 2 * blk, 2 * blk + 1
                PE.wait([z1, z2, z3, z5, z6, pf[2], pf[3]])
                lo, hi = slice(0, 64), slice(64, 128)
                mm(PS[lo, bank, col:col + 64], ck(fk, h, c0), ck(fq, h, c0), True, True)
                mm(PS[lo, bank, col + 64:col + 128], ck(fd, h, c0), ck(fq, h, c1), True, True)
                mm(PS[hi, bank, col:col + 64], ck(bd_, h, c1), ck(bq, h, c0), True, True)
                a = mm(PS[hi, bank, col + 64:col + 128], ck(fk, h, c1), ck(fq, h, c1), True, True, inc=(n in (3, 7)))
                if n == 3:
                    a0 = a
        a1 = a
        PE.wait([z4_, pf[4]])
        for h in range(4):
            for blk in range(2):
                n = 2 * h + blk
                for c, rows in ((0, slice(0, 64)), (1, slice(64, 128))):
                    a = mm(PS[rows, 4, 64 * n:64 * n + 64], ck(bk, h, 2 * blk + c), ck(bq, h, 2 * blk + c),
                           True, True, inc=(n == 7 and c == 1))
        a2 = a
        u = [tt(DV, h2(kf2, 0), hv(fd, 0), tv(totf, 1), ALU.mult, z1, z2, z3, z4_, z5, z6, x1),
             tt(DV, h2(qf2, 1), hv(fq, 3), tv(totf, 2), ALU.mult),
             tt(DV, h2(kb2, 1), hv(bd_, 3), tv(totb, 2), ALU.mult, x2, y["fk"], y["bd"]),
             tt(DV, h2(qb2, 0), hv(bq, 0), tv(totb, 1), ALU.mult),
             act(h2(kf2, 1), hv(fd, 1), ACT.Copy, z2, z3, z4_, z6),
             act(h2(qf2, 0), hv(fq, 2), ACT.Copy, z1),
             act(h2(kb2, 0), hv(bd_, 2), ACT.Copy, z6),
             act(h2(qb2, 1), hv(bq, 1), ACT.Copy, z5)]
        w1 = act(SCm[:, 0:512], PS[:, 2, :], ACT.Copy, a0, z5, z1)
        w2 = act(SCm[:, 512:1024], PS[:, 3, :], ACT.Copy, a1)
        pf[2] = [w1]
        pf[3] = [w2]
        mk = con("after64").bitcast(U32)
        for c, rows in ((0, slice(0, 64)), (1, slice(64, 128))):
            o = v3(SCm, 8)[rows, :, 64 * c:64 * c + 64]
            m_ = mk[rows, :].unsqueeze(1).to_broadcast([64, 8, 64])
            s_ = v3(PS[rows, 4, :], 8)
            w5 = DV.do(lambda e, o=o, m_=m_, s_=s_: e.copy_predicated(o, m_, s_), w1, w2, a2)
        pf[4] = [w5]
        go(1)
        PE.wait([*u, pf[5], pf[6]])
        for h in range(4):
            mm(PS[:, 5, 128 * h:128 * h + 128], kf2[:, 128 * h:128 * h + 128], qf2[:, 128 * h:128 * h + 128], True, True)
            a3 = mm(PS[:, 6, 128 * h:128 * h + 128], kb2[:, 128 * h:128 * h + 128], qb2[:, 128 * h:128 * h + 128],
                    True, True, inc=(h == 3))
        w3 = act(SF, PS[:, 5, :], ACT.Copy, a3, zt)
        w4 = act(SB, PS[:, 6, :], ACT.Copy, s2)
        pf[5] = [w3]
        pf[6] = [w4]
        go(1)
        SC8, SF4, SB4 = v3(SCm, 8), v3(SF, 4), v3(SB, 4)
        V = v3(v, 2)
        o_t = []
        PE.wait([w5, w3, w4, y["v"]])
        for half in range(2):
            t = []
            for tb in range(2):
                bank = 2 + 2 * half + tb
                PE.wait(pf[bank])
                for j in range(2):
                    h = 2 * half + j
                    o = PS[:, bank, 256 * j:256 * j + 256]
                    mm(o, SC8[:, 2 * h + tb, :], V[:, tb, 256 * h:256 * h + 256], True, False)
                    side = SB4 if tb == 0 else SF4
                    a = mm(o, side[:, h, :], V[:, 1 - tb, 256 * h:256 * h + 256], False, True, inc=(j == 1))
                t.append(a)
            o_t.append(t)
        go(4)
        gate = lambda tb, h: v3(r, 2)[:, tb, 256 * h:256 * h + 256]
        ot = []
        for half in range(2):
            b = norm_half((2 + 2 * half, 3 + 2 * half), half, 2, o_t[half], gate, [y["r2"], y["r"]])
            dst = tuple(x[:, 4 * half:4 * half + 4, :] for x in O)
            ot.append(turn(HS[:, :, 512 * half:512 * half + 512], 4, dst, None, [6, 7], [], lambda k, b=b: b))
        return Joined(*ot)

    def swiglu(layer, xt, pt):
        def up(i, of):
            b1, b2 = (2 * i) % 4, (2 * i + 1) % 4
            a1 = feat(f"ffn_w_in{layer}", 256 * i, b1, X, xt)
            a2 = feat(f"ffn_w_in{layer}", 2816 + 256 * i, b2, X)
            w = ar(512 * (i % 2), 512)
            a1 = act(w, PS[:, b1, :], ACT.Silu, a1)
            a = tt(DV, w, w, PS[:, b2, :], ALU.mult, a1, a2)
            pf[b1] = [a1]
            pf[b2] = [a]
            hi, lo = halves(i)
            c1_ = act(hi, w, ACT.Copy, a, of)
            return [c1_, tt(DV, lo, w, hi.bitcast(F32), ALU.subtract, c1_)]
        table(SILU)
        a = ffn(11, up, f"ffn_w_out{layer}")
        table(LOGEXP)
        ht = residual([4, 5, 6, 7], a)
        a = down(f"ple_w_proj{layer}", 0, pair("PT", 2, 0), 0, [0, 1, 2, 3], True, True, pt)
        return ht, a

    def load_p(layer):
        P = ar(1024, 512)
        dp = SP.dma(lambda e: e.dma_start(P.rearrange("p (b d) -> p b d", b=2),
                                          io["p"][layer * 256:layer * 256 + 256, :].rearrange("(b p) d -> p b d", p=128)),
                    hw["d_p"], 16 * (layer + 1), [DV.here(), AC.here(), PE.here()])
        return P, dp

    def ple(layer, ht, pa):
        pw, g = ar(1536, 2048), ar(3584, 2048)
        xt = norm_turn(ht, sml(f"pn{layer}"), PE.here(), range(4, 8))
        for tb in range(2):
            for n in range(2):
                b = 2 * tb + n
                e = act(pw[:, 1024 * tb + 512 * n:1024 * tb + 512 * n + 512], PS[:, b, :], ACT.Copy, pa[tb])
                pf[b] = [e]
        table(SIGMOID)
        t = [[], []]
        for n in range(4):
            b = n
            a = toks(f"ple_w_gate{layer}", 256 * n, b, X, xt)
            gg = v3(g, 2)[:, :, 256 * n:256 * n + 256]
            a = act(gg, v3(PS[:, b, :], 2), ACT.Sigmoid, a)
            pf[b] = [a]
            a = tt(DV, gg, gg, v3(pw, 2)[:, :, 256 * n:256 * n + 256], ALU.mult, a, e)
            a = tt(DV, H[:, :, 256 * n:256 * n + 256], H[:, :, 256 * n:256 * n + 256], gg, ALU.add, a, xt[7])
            if n % 2:
                t[0].append(a)
                t[1].append(a)
        table(LOGEXP)
        return t

    def diff(ht):
        xt = norm_turn(ht, sml("nm1"), PE.here())
        w, ls = fresh(64), fresh(4)
        for i in range(2):
            a = tt(DV, w, sml(f"lq{i + 1}"), sml(f"lk{i + 1}"), ALU.mult, DV.here())
            a = DV.do(lambda e, i=i: e.tensor_reduce(ls[:, i:i + 1], w, AX, ALU.add), a)
        a = act(ls[:, 0:2], ls[:, 0:2], ACT.Exp, a)
        nlam = ls[:, 2:3]
        a = tt(DV, ls[:, 3:4], ls[:, 1:2], ls[:, 0:1], ALU.subtract, a)
        lt = ts(DV, nlam, ls[:, 3:4], -LAMBDA_INIT, None, ALU.add, None, a)
        tabs = ar(0, 2048)
        PO.wait([DV.here(), AC.here(), d_con, d_sml])
        for qi, gname in enumerate(("gq", "gk")):
            g = sml(gname).rearrange("p (m a j) -> p m a j", m=2, a=2)
            for tb in range(2):
                for x in range(4):
                    tbl = con("cos" if x in (0, 2) else "sin")[:, 32 * tb:32 * tb + 32].unsqueeze(1).to_broadcast([128, 2, 32])
                    for h in range(2):
                        at = 512 * x + 256 * qi + 128 * tb + 64 * h
                        tabt = tt(PO, v3(tabs[:, at:at + 64], 2), g[:, :, (0, 1, 1, 0)[x], :], tbl, ALU.mult)
        tab = [tabs[:, 512 * x:512 * x + 512].rearrange("p (n j) -> p n j", j=32) for x in range(4)]
        v = ar(2048, 2048)
        S_ = [ar(4096 + 1024 * i, 1024) for i in range(2)]
        w1, w2 = ar(6144, 1024), ar(7168, 1024)
        QK = [ar(8192 + 1024 * i, 1024) for i in range(2)]
        Pm = [ar(10240 + 1024 * i, 1024) for i in range(2)]
        AT = [ar(12288 + 512 * i, 512) for i in range(2)]
        Aa = [ar(13312 + 512 * i, 512) for i in range(2)]
        mx, rs, cf = fresh(32), fresh(32), fresh(32)
        V = v3(v, 2)
        ev, sh, qk, s1, s3, s4, s5, s2 = {}, {}, {}, {}, {}, {}, {}, {}
        o_t, ot = [None, None], []
        bn = [0]
        TRB = (4, 7)

        def chunk(g, sec):
            b = bn[0] % 2
            bn[0] += 1
            a = toks("diff_w_in", sec * 1024 + 256 * g, b, X, xt)
            o = (v3(S_[g % 2][:, 512 * sec:512 * sec + 512], 2) if sec < 2
                 else V[:, :, 256 * g:256 * g + 256])
            x = act(o, v3(PS[:, b, :], 2), ACT.Copy, a, qk.get(("t", g - 2)))
            pf[b] = [x]
            ev[(g, sec)] = x

        def shape1(g):
            S = S_[g % 2]
            ss = fresh(16)
            a = act(w1, S, ACT.Square, ev[(g, 0)], ev[(g, 1)], sh.get(g - 1))
            a = DV.do(lambda e: e.tensor_reduce(ss, v3(w1, 16), AX, ALU.add), a)
            r, a = rstd(ss, 16, 1.0 / 64, a)
            a = tt(DV, v3(S, 16), v3(S, 16), r.unsqueeze(2).to_broadcast([128, 16, 64]), ALU.mult, a)
            c = lambda ap, h: ap.rearrange("p (n a j) -> p n a j", a=2, j=32)[:, :, h, :]
            p = [tt(PO, c(w2, 0), c(S, 1), tab[1], ALU.mult, a, tabt, sh.get(g - 1)),
                 tt(PO, c(w2, 1), c(S, 0), tab[3], ALU.mult),
                 tt(DV, c(w1, 0), c(S, 0), tab[0], ALU.mult, tabt, a),
                 tt(DV, c(w1, 1), c(S, 1), tab[2], ALU.mult)]
            b1 = tt(DV, c(S, 0), c(w1, 0), c(w2, 0), ALU.subtract, p)
            sh[g] = [b1, tt(DV, c(S, 1), c(w1, 1), c(w2, 1), ALU.add, p)]

        def shape2(g):
            S = S_[g % 2]
            for qi in range(2):
                bank = TRB[qi]
                PE.wait([sh[g], pf[bank]])
                for j in range(2):
                    for tb in range(2):
                        a = tr(PS[:, bank, 256 * j + 128 * tb:256 * j + 128 * tb + 128],
                               S[:, 512 * qi + 256 * tb + 128 * j:512 * qi + 256 * tb + 128 * j + 128],
                               inc=(j == 1 and tb == 1))
                qk[("t", g)] = a
                o = QK[g % 2][:, 512 * qi:512 * qi + 512]
                if qi:
                    e = act(o, PS[:, bank, :], ACT.Copy, a, qk.get(("s", g - 2)))
                else:
                    e = DV.do(lambda e, o=o, bank=bank: e.tensor_copy(o, PS[:, bank, :]), a, qk.get(("s", g - 2)))
                pf[bank] = [e]
                qk[(g, qi)] = e

        def A(h):
            g = h // 2
            Q, K = (v3(QK[g % 2][:, 512 * i:512 * i + 512], 2) for i in range(2))
            PE.wait([qk[(g, 0)], qk[(g, 1)]])
            for m in range(2):
                bk = 2 + m
                rows = slice(64 * m, 64 * m + 64)
                for tb in range(2):
                    a = mm(PS[:, bk, 256 * tb:256 * tb + 256], Q[rows, h % 2, 128 * tb:128 * tb + 128],
                           K[rows, h % 2, :], True, True, pf[bk], inc=(tb == 1))
                if m:
                    qk[("s", g)] = a
                c = 4 * h + 2 * m
                x = DV.do(lambda e, c=c, bk=bk: e.tensor_reduce(mx[:, c:c + 2], v3(PS[:, bk, :], 2), AX, ALU.max), a)
                x = ts(DV, mx[:, c:c + 2], mx[:, c:c + 2], -0.125, None, ALU.mult, None, x)
                for tb in range(2):
                    o = Pm[h % 2][:, 512 * m + 256 * tb:512 * m + 256 * tb + 256]
                    yx = act(o, PS[:, bk, 256 * tb:256 * tb + 256], ACT.Exp, x, s3.get(h - 2), bias=mx[:, c + tb:c + tb + 1],
                             scale=0.125, accum_out=rs[:, c + tb:c + tb + 1])
                pf[bk] = [yx]
            s1[h] = yx

        def B(h):
            c = 4 * h
            x = DV.do(lambda e: e.reciprocal(cf[:, c:c + 4], rs[:, c:c + 4]), s1[h])
            x = ts(DV, cf[:, c + 2:c + 4], cf[:, c + 2:c + 4], nlam, None, ALU.mult, None, x, lt)
            for tb in range(2):
                o = Aa[h % 2][:, 256 * tb:256 * tb + 256]
                p0 = Pm[h % 2][:, 256 * tb:256 * tb + 256]
                p1 = Pm[h % 2][:, 512 + 256 * tb:512 + 256 * tb + 256]
                yx = ts(DV, o, p1, cf[:, c + 2 + tb:c + 3 + tb], None, ALU.mult, None, x, s4.get(h - 2))
                yx = stt(o, p0, cf[:, c + tb:c + tb + 1], o, ALU.mult, ALU.add, yx)
            s3[h] = yx

        def C(h):
            bank = TRB[h % 2]
            PE.wait([s3[h], pf[bank]])
            for sb_ in range(2):
                for tb in range(2):
                    a = tr(PS[:, bank, 256 * sb_ + 128 * tb:256 * sb_ + 128 * tb + 128],
                           Aa[h % 2][:, 256 * tb + 128 * sb_:256 * tb + 128 * sb_ + 128], inc=(sb_ == 1 and tb == 1))
            s4[h] = a
            e = act(AT[h % 2], PS[:, bank, :], ACT.Copy, a, s5.get(h - 2))
            pf[bank] = [e]
            s2[h] = e

        def Dd(h):
            at_ = v3(AT[h % 2], 2)
            PE.wait([s2[h], ev[(h // 2, 2)]])
            for tb in range(2):
                bank = 5 + tb
                if h % 4 == 0:
                    PE.wait(pf[bank])
                o = PS[:, bank, 128 * (h % 4):128 * (h % 4) + 128]
                mm(o, at_[:, 0, 128 * tb:128 * tb + 128], V[:, 0, 128 * h:128 * h + 128], True, False)
                a = mm(o, at_[:, 1, 128 * tb:128 * tb + 128], V[:, 1, 128 * h:128 * h + 128], False, True, inc=True)
                o_t[tb] = a
            s5[h] = a
            if h % 4 == 3:
                half = h // 4
                b = norm_half((5, 6), half, 4, list(o_t), lambda tb, h: sml("gsub"), None, scale=1.0 - LAMBDA_INIT)
                halves_.append(b)

        halves_ = []

        def tail(half):
            dst = tuple(x[:, 4 * half:4 * half + 4, :] for x in O)
            b = halves_[half]
            ot.append(turn(HS[:, :, 512 * half:512 * half + 512], 4, dst, None, [4, 7], [], lambda k: b))

        def att1(i):
            if 0 <= i - 1 < 8:
                B(i - 1)
            if 0 <= i < 8:
                A(i)

        def att2(i):
            if 0 <= i - 2 < 8:
                Dd(i - 2)
            if 0 <= i - 1 < 8:
                C(i - 1)

        def run(*steps):
            for f, *x in steps:
                f(*x)

        run((chunk, 0, 0), (chunk, 0, 1), (shape1, 0), (chunk, 0, 2), (chunk, 1, 0), (shape2, 0), (chunk, 1, 1),
            (att1, 0), (shape1, 1), (chunk, 2, 0), (att2, 0),
            (att1, 1), (shape2, 1), (chunk, 2, 1), (att2, 1),
            (att1, 2), (shape1, 2), (chunk, 1, 2), (att2, 2),
            (att1, 3), (shape2, 2), (chunk, 3, 0), (att2, 3),
            (att1, 4), (chunk, 3, 1), (att2, 4),
            (att1, 5), (shape1, 3), (chunk, 2, 2), (att2, 5), (shape2, 3),
            (att1, 6), (chunk, 3, 2), (att2, 6),
            (att1, 7), (tail, 0), (lambda: ot[0][3],), (att2, 7), (att1, 8), (att2, 8), (att2, 9))
        tail(1)
        return Joined(*ot)

    if stage >= 2:
        ot = gla()
        ht = project("gla_w_out", O, ot, [0, 1, 2, 3])
    for layer in range(2):
        if stage < 3 + layer:
            break
        if layer == 1:
            ot = diff(ht)
            ht = project("diff_w_out", O, ot, [0, 1, 2, 3])
        P, dp = load_p(layer)
        xt = norm_turn(ht, sml(f"nf{layer}"), PE.here(), range(4, 8))
        pt = turn(v3(P, 2), 2, pair("PT", 2, 0), None, [0, 1], PE.here(), lambda k: dp)
        ht, pa = swiglu(layer, xt, pt)
        ht = ple(layer, ht, pa)
    e = SP.dma(lambda e: e.dma_start(out.rearrange("(b p) d -> p b d", p=128), H), hw["d_out"], 16, ht)
    SP.wait([e])
    return {"SP": SP, "ACT": AC, "DVE": DV, "POOL": PO, "PE": PE}


STREAMED = {"w_in": "w_in", "w_o_sb": "w_o_sb", "w_o_hg": "w_o_hg", "w_out": "w_out", "w_ff1": "w_ff1",
            "w_ff2": "w_ff2", "gla_w_in": "gla_w_in_2", "gla_w_out": "gla_w_out_2",
            "diff_w_in": "diff_w_in_2", "diff_w_out": "diff_w_out_2"}
LAYERED = {"ffn_w_in": "ffn_w_in_2", "ffn_w_out": "ffn_w_out_2", "ple_w_gate": "ple_w_gate_2",
           "ple_w_proj": "ple_w_proj_2"}
STAGE = 4


def kernel(**inputs):
    import concourse.bacc as _bacc
    from concourse.bass_utils import run_bass_kernel_spmd as _run

    nc = _bacc.Bacc("TRN2", target_bir_lowering=False, num_devices=1)
    arrays, io = {}, {}

    def give(name, a):
        a = np.ascontiguousarray(a)
        arrays[f"in_{name}_dram"] = a
        io[name] = nc.dram_tensor(f"in_{name}_dram", a.shape, mybir.dt.from_np(a.dtype), kind="ExternalInput").ap()

    I = {k: np.asarray(v) for k, v in inputs.items()}
    for name, key in STREAMED.items():
        give(name, I[key][0])
    for name, key in LAYERED.items():
        for layer in range(2):
            give(f"{name}{layer}", I[key][layer])
    give("x", I["x"][0])
    give("p", I["p_2"].reshape(512, 256))
    give("const", constants()[0])
    col = lambda a: a.reshape(-1, 128).T
    row = lambda a: np.broadcast_to(a.reshape(1, -1), (128, a.size))
    small = {
        "g1": col(I["norm1_g"]), "g2": col(I["norm2_g"]), "bg": col(I["b_gate"]),
        "lb0": col(I["lb_logits"][0]), "lb1": col(I["lb_logits"][1]),
        "nm0": col(I["norm_mix_2"][0]), "nm1": col(I["norm_mix_2"][1]),
        "nf0": col(I["norm_ffn_2"][0]), "nf1": col(I["norm_ffn_2"][1]),
        "pn0": col(I["ple_norm_2"][0]), "pn1": col(I["ple_norm_2"][1]),
        "gbf": col(I["gla_b_gate_f_2"]), "gbb": col(I["gla_b_gate_b_2"]),
        "hgg": row(I["hg_norm_g"]), "gog": row(I["gla_g_out_2"]), "gq": row(I["diff_g_q_2"]),
        "gk": row(I["diff_g_k_2"]), "gsub": row(I["diff_g_sub_2"]), "lq1": row(I["diff_lam_q1_2"]),
        "lk1": row(I["diff_lam_k1_2"]), "lq2": row(I["diff_lam_q2_2"]), "lk2": row(I["diff_lam_k2_2"]),
    }
    give("small", np.concatenate([small[k] for k, _ in SMALL], axis=1))
    give("final", row(I["final_g"]))
    give("wgate", np.concatenate([I["gla_w_gate_f_2"][0], I["gla_w_gate_b_2"][0]], axis=1))
    out = nc.dram_tensor("out_0_dram", (256, 1024), F32, kind="ExternalOutput").ap()
    program(nc, io, out, STAGE)
    r = _run(nc, [arrays], core_ids=[0])
    return r.results[0]["out_0_dram"].reshape(1, 256, 1024)
```
